# Optimizing a Trainium2 kernel written in Bass

```python
import jax, jax.numpy as jnp
from jax import lax
import numpy as np

D_MODEL = 2048
BATCH = 1
SEQ = 256
DEPTH = 2

HEAD_DIM = 128
N_MIX_HEADS = D_MODEL // HEAD_DIM
A_HEADS = N_MIX_HEADS // 4
B_HEADS = (N_MIX_HEADS - A_HEADS) // 2
C_HEADS = N_MIX_HEADS - A_HEADS - B_HEADS
C_KV_HEADS = 2
A_KEY_DIM = 128
A_CHUNK = 16
DILATED_PATTERNS = ((128, 1), (512, 4), (2048, 16))
C_WINDOW = 128
BLOCK = 128
ROPE_THETA = 500000.0
ROPE_DIM = HEAD_DIM // 4
D_FF = 5632
CONV_WIDTH = 3
LN_EPS = 1e-5
ALPHA = (2 * DEPTH) ** 0.25
BETA = (8 * DEPTH) ** -0.25

A_KEY_WIDTH = A_HEADS * A_KEY_DIM
A_WIDTH = A_HEADS * HEAD_DIM
B_WIDTH = B_HEADS * HEAD_DIM
C_WIDTH = C_HEADS * HEAD_DIM
C_KV_WIDTH = C_KV_HEADS * HEAD_DIM
MIX_WIDTH = A_WIDTH + B_WIDTH + C_WIDTH
PROJ_SIZES = (A_KEY_WIDTH, A_KEY_WIDTH, A_WIDTH, A_WIDTH,
              B_WIDTH, B_WIDTH, B_WIDTH,
              C_WIDTH, C_KV_WIDTH, C_KV_WIDTH)
VALUE_BLOCKS = (2, 6, 9)
IN_WIDTH = sum(PROJ_SIZES)

kernel_name = "hybrid_hgrn2_dilated_swa_sink_convffn"

def layer_norm(x, g, b):
    xf = x.astype(jnp.float32)
    mu = jnp.mean(xf, -1, keepdims=True)
    var = jnp.mean(jnp.square(xf - mu), -1, keepdims=True)
    return ((xf - mu) * lax.rsqrt(var + LN_EPS) * g.astype(jnp.float32) + b.astype(jnp.float32)).astype(x.dtype)

def rms_norm(x, g):
    xf = x.astype(jnp.float32)
    return xf * lax.rsqrt(jnp.mean(jnp.square(xf), -1, keepdims=True) + LN_EPS) * g.astype(jnp.float32)

def rope_tables(seq):
    inv = ROPE_THETA ** (-jnp.arange(0, ROPE_DIM, 2, dtype=jnp.float32) / ROPE_DIM)
    ang = jnp.arange(seq, dtype=jnp.float32)[:, None] * inv[None, :]
    return jnp.cos(ang), jnp.sin(ang)

def partial_rope(x, cos, sin):
    half = ROPE_DIM // 2
    xr = x[..., :ROPE_DIM].astype(jnp.float32)
    x1, x2 = xr[..., :half], xr[..., half:]
    rot = jnp.concatenate([x1 * cos - x2 * sin, x2 * cos + x1 * sin], -1)
    return jnp.concatenate([rot.astype(x.dtype), x[..., ROPE_DIM:]], -1)

def banded_attention(q, k, v, max_lag, sink=None):
    b, h, L, dh = q.shape
    nb = -(-L // BLOCK)
    pad = nb * BLOCK - L
    padw = ((0, 0), (0, 0), (0, pad), (0, 0))
    qb = jnp.pad(q, padw).reshape(b, h, nb, BLOCK, dh)
    kb = jnp.pad(k, padw).reshape(b, h, nb, BLOCK, dh)
    vb = jnp.pad(v, padw).reshape(b, h, nb, BLOCK, dh)
    shift = ((0, 0), (0, 0), (1, 0), (0, 0), (0, 0))
    kk = jnp.concatenate([jnp.pad(kb, shift)[:, :, :-1], kb], axis=3)
    vv = jnp.concatenate([jnp.pad(vb, shift)[:, :, :-1], vb], axis=3)
    s = jnp.einsum('bhnqd,bhnkd->bhnqk', qb, kk, preferred_element_type=jnp.float32) * (dh ** -0.5)
    r = jnp.arange(BLOCK)[:, None]
    c = jnp.arange(2 * BLOCK)[None, :]
    lag = BLOCK + r - c
    kpos = (jnp.arange(nb)[:, None, None] - 1) * BLOCK + c[None]
    valid = ((lag >= 0) & (lag <= max_lag))[None] & (kpos >= 0)
    s = jnp.where(valid, s, -jnp.inf)
    m = jnp.max(s, -1)
    if sink is not None:
        sk = sink.astype(jnp.float32)[None, :, None, None]
        m = jnp.maximum(m, sk)
    e = jnp.exp(s - m[..., None])
    denom = jnp.sum(e, -1)
    if sink is not None:
        denom = denom + jnp.exp(sk - m)
    out = jnp.einsum('bhnqk,bhnkd->bhnqd', e, vv.astype(jnp.float32)) / denom[..., None]
    lse = m + jnp.log(denom)
    out = out.reshape(b, h, nb * BLOCK, dh)[:, :, :L].astype(q.dtype)
    return out, lse.reshape(b, h, nb * BLOCK)[:, :, :L]

def dilated_attention(q, k, v):
    b, h, S, dh = q.shape
    outs, lses = [], []
    for window, dil in DILATED_PATTERNS:
        L = S // dil
        def split(t):
            return t.reshape(b, h, L, dil, dh).transpose(0, 1, 3, 2, 4).reshape(b, h * dil, L, dh)
        o, lse = banded_attention(split(q), split(k), split(v), window // dil)
        outs.append(o.reshape(b, h, dil, L, dh).transpose(0, 1, 3, 2, 4).reshape(b, h, S, dh))
        lses.append(lse.reshape(b, h, dil, L).transpose(0, 1, 3, 2).reshape(b, h, S))
    w = jax.nn.softmax(jnp.stack(lses, 0), axis=0)
    out = jnp.einsum('pbhs,pbhsd->bhsd', w, jnp.stack(outs, 0).astype(jnp.float32))
    return out.astype(q.dtype)

def hgrn2(q, f_logit, i, g, lb, norm_w):
    b, S, _ = q.shape
    n = S // A_CHUNK
    def chunks(t, dim):
        return t.astype(jnp.float32).reshape(b, n, A_CHUNK, A_HEADS, dim).transpose(0, 3, 1, 2, 4)
    qc = jax.nn.silu(chunks(q, A_KEY_DIM))
    fg = lb.astype(jnp.float32).reshape(A_HEADS, 1, 1, A_KEY_DIM) + \
        (1.0 - lb.astype(jnp.float32).reshape(A_HEADS, 1, 1, A_KEY_DIM)) * jax.nn.sigmoid(chunks(f_logit, A_KEY_DIM))
    kc = 1.0 - fg
    vc = chunks(i, HEAD_DIM)
    bcum = jnp.cumsum(jnp.log(fg), axis=3)
    causal = jnp.tril(jnp.ones((A_CHUNK, A_CHUNK), dtype=bool))
    diff = bcum[:, :, :, :, None, :] - bcum[:, :, :, None, :, :]
    decay = jnp.exp(jnp.where(causal[:, :, None], diff, -jnp.inf))
    att = jnp.einsum('bhnik,bhnjk,bhnijk->bhnij', qc, kc, decay)
    o_intra = jnp.einsum('bhnij,bhnjv->bhniv', att, vc)
    blast = bcum[:, :, :, -1:, :]
    upd = jnp.einsum('bhnck,bhncv->bhnkv', kc * jnp.exp(blast - bcum), vc)
    cdec = jnp.exp(blast[:, :, :, 0, :])
    def step(state, inp):
        dec, u = inp
        return dec[..., None] * state + u, state
    s0 = jnp.zeros((b, A_HEADS, A_KEY_DIM, HEAD_DIM), jnp.float32)
    _, s_prev = lax.scan(step, s0, (jnp.moveaxis(cdec, 2, 0), jnp.moveaxis(upd, 2, 0)))
    s_prev = jnp.moveaxis(s_prev, 0, 2)
    o_inter = jnp.einsum('bhnck,bhnkv->bhncv', qc * jnp.exp(bcum), s_prev)
    o = (o_intra + o_inter).transpose(0, 2, 3, 1, 4).reshape(b, S, A_HEADS, HEAD_DIM)
    o = rms_norm(o, norm_w).reshape(b, S, A_WIDTH)
    return (o * jax.nn.silu(g.astype(jnp.float32))).astype(q.dtype)

def mixer_sublayer(x, w_in, lb, a_norm_w, c_sink, w_out, cos, sin):
    b, S, _ = x.shape
    proj = x @ w_in
    idx = [int(t) for t in np.cumsum(PROJ_SIZES)[:-1]]
    qA, fA, iA, gA, qB, kB, vB, qC, kC, vC = jnp.split(proj, idx, axis=-1)
    def heads(t, nh):
        return t.reshape(b, S, nh, HEAD_DIM).transpose(0, 2, 1, 3)
    def merge(t):
        return t.transpose(0, 2, 1, 3).reshape(b, S, -1)
    oA = hgrn2(qA, fA, iA, gA, lb, a_norm_w)
    oB = dilated_attention(partial_rope(heads(qB, B_HEADS), cos, sin),
                           partial_rope(heads(kB, B_HEADS), cos, sin), heads(vB, B_HEADS))
    rep = C_HEADS // C_KV_HEADS
    kCh = jnp.repeat(partial_rope(heads(kC, C_KV_HEADS), cos, sin), rep, axis=1)
    vCh = jnp.repeat(heads(vC, C_KV_HEADS), rep, axis=1)
    oC, _ = banded_attention(partial_rope(heads(qC, C_HEADS), cos, sin), kCh, vCh, C_WINDOW - 1, c_sink)
    mixed = jnp.concatenate([oA, merge(oB), merge(oC)], axis=-1)
    return mixed @ w_out

def conv_ffn(x, w_gate, w_up, conv_w, conv_b, w_down):
    S = x.shape[1]
    g = x @ w_gate
    u = x @ w_up
    gp = jnp.pad(g, ((0, 0), (CONV_WIDTH - 1, 0), (0, 0)))
    gc = conv_b
    for j in range(CONV_WIDTH):
        gc = gc + conv_w[j] * gp[:, j:j + S]
    return (jax.nn.silu(gc) * u) @ w_down

def setup_inputs(seed: int = 0) -> dict:
    key = jax.random.key(seed)
    ks = jax.random.split(key, 24)
    f32 = jnp.float32
    x = jax.random.normal(ks[0], (BATCH, SEQ, D_MODEL), f32)
    blocks = []
    for j, size in enumerate(PROJ_SIZES):
        w = jax.random.normal(ks[1 + j], (DEPTH, D_MODEL, size), f32) * D_MODEL ** -0.5
        if j in VALUE_BLOCKS:
            w = w * BETA
        blocks.append(w)
    w_in = jnp.concatenate(blocks, axis=-1)
    lb_logits = jax.random.normal(ks[11], (DEPTH, A_KEY_WIDTH), f32)
    a_norm_w = 1.0 + 0.02 * jax.random.normal(ks[12], (DEPTH, HEAD_DIM), f32)
    c_sinks = jax.random.normal(ks[13], (DEPTH, C_HEADS), f32)
    w_out = jax.random.normal(ks[14], (DEPTH, MIX_WIDTH, D_MODEL), f32) * (MIX_WIDTH ** -0.5) * BETA
    ln1_g = 1.0 + 0.02 * jax.random.normal(ks[15], (DEPTH, D_MODEL), f32)
    ln1_b = 0.02 * jax.random.normal(ks[16], (DEPTH, D_MODEL), f32)
    w_gate = jax.random.normal(ks[17], (DEPTH, D_MODEL, D_FF), f32) * D_MODEL ** -0.5
    w_up = jax.random.normal(ks[18], (DEPTH, D_MODEL, D_FF), f32) * (D_MODEL ** -0.5) * BETA
    conv_w = jax.random.normal(ks[19], (DEPTH, CONV_WIDTH, D_FF), f32) * CONV_WIDTH ** -0.5
    conv_b = 0.02 * jax.random.normal(ks[20], (DEPTH, D_FF), f32)
    w_down = jax.random.normal(ks[21], (DEPTH, D_FF, D_MODEL), f32) * (D_FF ** -0.5) * BETA
    ln2_g = 1.0 + 0.02 * jax.random.normal(ks[22], (DEPTH, D_MODEL), f32)
    ln2_b = 0.02 * jax.random.normal(ks[23], (DEPTH, D_MODEL), f32)
    return {"x": x, "w_in": w_in, "lb_logits": lb_logits, "a_norm_w": a_norm_w, "c_sinks": c_sinks,
            "w_out": w_out, "ln1_g": ln1_g, "ln1_b": ln1_b, "w_gate": w_gate, "w_up": w_up,
            "conv_w": conv_w, "conv_b": conv_b, "w_down": w_down, "ln2_g": ln2_g, "ln2_b": ln2_b}

def reference(x, w_in, lb_logits, a_norm_w, c_sinks, w_out, ln1_g, ln1_b, w_gate, w_up,
              conv_w, conv_b, w_down, ln2_g, ln2_b):
    cos, sin = rope_tables(x.shape[1])
    lbs = jnp.cumsum(jax.nn.softmax(lb_logits.astype(jnp.float32), axis=0), axis=0)
    lbs = lbs - lbs[0]
    for l in range(DEPTH):
        y = mixer_sublayer(x, w_in[l], lbs[l], a_norm_w[l], c_sinks[l], w_out[l], cos, sin)
        x = layer_norm(ALPHA * x + y, ln1_g[l], ln1_b[l])
        y = conv_ffn(x, w_gate[l], w_up[l], conv_w[l], conv_b[l], w_down[l])
        x = layer_norm(ALPHA * x + y, ln2_g[l], ln2_b[l])
    return x


_drawn_inputs = setup_inputs


def setup_inputs(seed=0):
    import zlib

    import numpy as np

    out = dict(_drawn_inputs(seed))
    spreads = {}
    factors = {'lb_logits': 5.882, 'a_norm_w': 23.48, 'c_sinks': 31.86, 'conv_b': 8.0}
    for name, (base, spread) in spreads.items():
        noise = np.random.default_rng([zlib.crc32(name.encode()), seed]).standard_normal(out[name].shape)
        drawn = base * np.exp(spread * noise) if base else spread * noise
        out[name] = __import__('jax').numpy.asarray(drawn.astype(out[name].dtype))
    for name, factor in factors.items():
        out[name] = (out[name] * factor).astype(out[name].dtype)
    return out
```

```python
import math
from contextlib import ExitStack

import concourse.bass as bass
import numpy as np
from concourse import mybir

D_MODEL, SEQ, DEPTH, HEAD, D_FF, TAPS = 2048, 256, 2, 128, 5632, 3
A_HEADS, B_HEADS, C_HEADS, C_KV = 4, 6, 6, 2
PATTERNS, C_WINDOW = ((128, 1), (512, 4), (2048, 16)), 128
IN_WIDTH = (4 * A_HEADS + 3 * B_HEADS + C_HEADS + 2 * C_KV) * HEAD
ROPE_THETA, ROPE = 500000.0, HEAD // 4
EPS = 1e-5
ALPHA = (2 * DEPTH) ** 0.25
SCALE = HEAD ** -0.5
NEG = -1e30

P = 128
TT = SEQ // P
KT = D_MODEL // P
FT = D_FF // P
CW = 512
GK = 2
GC = KT // GK
GD = FT // GK
RING = 4
NC_IN, NC_OUT, NC_FF = IN_WIDTH // CW, D_MODEL // CW, D_FF // CW
BASE_OUT = NC_IN * GC
BASE_FFN = BASE_OUT + NC_OUT * GC
BASE_DOWN = BASE_FFN + 2 * NC_FF * GC
GROUPS = BASE_DOWN + NC_OUT * GD
LAYER_FILLS = GROUPS // RING
LAG = 3

F_CHUNK, Q_CHUNK, I_CHUNK, G_CHUNK = 1, 0, 2, 3
ORDER = [F_CHUNK, Q_CHUNK] + list(range(4, NC_IN)) + [I_CHUNK, G_CHUNK]
QB0 = 4 * A_HEADS
VB0 = QB0 + 2 * B_HEADS
QC0 = VB0 + B_HEADS
VC0 = QC0 + C_HEADS + C_KV


def qk_slot(block):
    if QB0 <= block < VB0:
        return block - QB0
    if QC0 <= block < VC0:
        return 2 * B_HEADS + block - QC0
    return None


def chunk_blocks(chunk):
    return range(4 * chunk, 4 * chunk + 4)


def parts(chunk):
    runs = []
    for name, b0, b1 in (("staged", 0, VB0), ("vB", VB0, QC0), ("staged", QC0, VC0), ("vC", VC0, 4 * NC_IN)):
        lo, hi = max(b0, 4 * chunk), min(b1, 4 * chunk + 4)
        if lo < hi:
            runs.append((name, lo, hi))
    return runs


def rope_blocks(chunk):
    return [b - 4 * chunk for b in chunk_blocks(chunk) if qk_slot(b) is not None]


def turned_pairs(chunk):
    if chunk in (F_CHUNK, Q_CHUNK):
        return [0, 1]
    return sorted({b // 2 for b in rope_blocks(chunk)})


LEVELS = 8
N_HEADS = B_HEADS + C_HEADS
MIX_ORDER = [2, 3, 4, 5, 6, 7, 0, 1]

WHEN = {("params", 0): GC + 1}
for i, chunk in enumerate(ORDER):
    WHEN["evac", i] = GC * i + 7
    if turned_pairs(chunk):
        WHEN["turn", i] = GC * (i + 1) + 3
for n in range(LEVELS + 1):
    WHEN["level", n] = 22 + 4 * n
for k in range(N_HEADS):
    at = 56 + 3 * k if k < B_HEADS else 76 + 2 * (k - B_HEADS)
    WHEN["score", k], WHEN["finish", k], WHEN["flip", k], WHEN["value", k] = at, at + 1, at + 2, at + 3
WHEN["hout", 0], WHEN["hsquare", 0], WHEN["hscale", 0] = 83, 84, 85
WHEN["hgate", 0], WHEN["hturn", 0] = 88, 90
for n in range(GC):
    WHEN["mixsplit", n] = BASE_OUT - 1 + n
for c in range(NC_OUT):
    WHEN["yevac", c] = BASE_OUT + GC * c + 7
KINDS = ["params", "evac", "turn", "level", "hout", "hsquare", "hscale", "flip", "value", "finish", "score",
         "hgate", "hturn", "mixsplit", "yevac"]
STEPS = {}
for (kind, k), at in sorted(WHEN.items(), key=lambda w: (w[1], KINDS.index(w[0][0]), w[0][1])):
    STEPS.setdefault(at, []).append((kind, k))
TURNS = [i for i in range(len(ORDER)) if ("turn", i) in WHEN]
ROPES = [i for i in TURNS if rope_blocks(ORDER[i])]
B_TURN = max(i for i in TURNS if chunk_blocks(ORDER[i])[0] < VB0 and rope_blocks(ORDER[i]))
C_TURN = max(TURNS)
I_AT, G_AT = ORDER.index(I_CHUNK), ORDER.index(G_CHUNK)
V_AT = max(i for i, chunk in enumerate(ORDER) if any(VB0 <= b < QC0 for b in chunk_blocks(chunk)))


def in_banks(i):
    return (0, 1) if i % 2 == 0 else (2, 3)


def out_banks(c):
    return in_banks(c + 1)


def bank_uses():
    uses = [[("xturn", 0)] for _ in range(8)]
    for p in range(BASE_FFN):
        if p % GC == 0:
            i = p // GC
            for b in in_banks(i) if p < BASE_OUT else out_banks(i - NC_IN):
                uses[b].append(("proj", i) if p < BASE_OUT else ("out", i - NC_IN))
        for kind, k in STEPS.get(p, ()):
            banks = {"params": (6,), "turn": None, "level": (6, 7) if k < LEVELS else (6,), "score": (6 + k % 2,),
                     "flip": (4,), "value": (5,), "hout": (6, 7), "hturn": (4, 5)}.get(kind, ())
            if kind == "turn":
                banks = [4 + pair for pair in turned_pairs(ORDER[k])]
            for b in banks:
                uses[b].append((kind, k))
    for b in range(8):
        uses[b].append(("xturn", 1))
    for c in range(NC_OUT):
        for b in in_banks(c):
            uses[b].append(("down", c))
    return uses


USES = bank_uses()
FULL = [[u for u in bank if u[0] not in ("proj", "out", "down")] for bank in USES]

PAR_LN = (2 * KT, 0)
PAR_CONV = 4 * KT
PAR_COLS = 4 * KT + (TAPS + 1) * FT
PAR_SETS = (4 * KT + FT, 2 * FT, FT)
ACT_LINKS, DVE_LINKS, POOL_LINKS, FFN_LINKS = 8, 55, 43, 8 * NC_FF
PAIRS = 2 * NC_FF


def program(nc, x, w_in, lb_logits, a_norm_w, c_sinks, w_out, ln1_g, ln1_b, w_gate, w_up, conv_w, conv_b,
            w_down, ln2_g, ln2_b, c_ident, c_bias, c_level, c_rope, c_unit, out):
    F32, F32R, U8 = mybir.dt.float32, mybir.dt.float32r, mybir.dt.uint8
    ACT, ALU, AX = mybir.ActivationFunctionType, mybir.AluOpType, mybir.AxisListType
    ctx = ExitStack()
    with ctx:
        def sb(name, shape, dt=F32):
            return ctx.enter_context(nc.sbuf_tensor(name, shape, dt))

        def sem(name):
            return ctx.enter_context(nc.semaphore(name))

        raw = sb("raw", [P, RING, GK, CW])
        whi = sb("whi", [P, RING, GK, CW], F32R)
        wlo = sb("wlo", [P, RING, GK, CW], F32R)
        xT = sb("xT", [P, KT, 2, SEQ], F32R)
        xres = sb("xres", [P, TT, D_MODEL])
        mix = sb("mix", [P, KT, SEQ])
        flat = mix[:, :, :].rearrange("p k s -> p (k s)")
        lnb = flat.rearrange("p (a d) -> p a d", a=2)
        fsum = flat[:, 0:1024].rearrange("p (q m s) -> p q m s", q=2, m=2)
        fconv = flat[:, 1024:2048].rearrange("p (q m s) -> p q m s", q=2, m=2)
        fsilu = flat[:, 2048:3072].rearrange("p (q m s) -> p q m s", q=2, m=2)
        ident = sb("ident", [P, P])
        parT = sb("parT", [P, PAR_COLS])
        conv = parT[:, PAR_CONV:].rearrange("p (a f) -> p a f", f=FT)
        parC = sb("parC", [P, TAPS + 1, 4])
        rope = sb("rope", [P, 2, TT, ROPE])
        sinks = sb("sinks", [P, N_HEADS])
        lbw = sb("lbw", [P, 6, DEPTH, A_HEADS])
        lbc = sb("lbc", [P, 2, 1, A_HEADS])
        stats = sb("stats", [P, TT, NC_OUT, 6])
        mv = sb("mv", [P, TT, 2])
        lns = sb("lns", [P, 3, TT])
        hd = sb("hd", [P, 2, 5, TT])
        hs = sb("hs", [P, 4, TT * A_HEADS])
        anorm = sb("anorm", [P, HEAD])
        spare = sb("spare", [P, 6 + 2 * LEVELS])
        arena_base = (nc.sbuf_base + 31) // 32 * 32
        ctx.enter_context(nc.sbuf_tensor("arena", [P, FT * 2 * SEQ], F32))
        hT = nc.alloc_sbuf_tensor_at("hT", [P, FT, 2, SEQ], F32R, offset=arena_base)
        place = [arena_base]

        def at(name, shape, dt=F32, size=4):
            t = nc.alloc_sbuf_tensor_at(name, shape, dt, offset=place[0])
            place[0] += int(np.prod(shape[1:])) * size
            assert place[0] <= arena_base + FT * 2 * SEQ * 4, place[0] - arena_base
            return t

        qT = at("qT", [P, A_HEADS, SEQ])
        kT = at("kT", [P, A_HEADS, SEQ])
        pre = at("pre", [P, A_HEADS, SEQ])
        suf = at("suf", [P, A_HEADS, SEQ])
        ql = at("ql", [P, A_HEADS, SEQ])
        kl = at("kl", [P, A_HEADS, SEQ])
        att = at("att", [P, A_HEADS * TT, P])
        att01 = at("att01", [P, A_HEADS, P])
        iA = at("iA", [P, TT, CW])
        gA = at("gA", [P, TT, CW])
        qkT = at("qkT", [P, 2 * B_HEADS + C_HEADS + C_KV, SEQ])
        vB = at("vB", [P, TT, B_HEADS * HEAD])
        vC = at("vC", [P, TT, C_KV * HEAD])
        staged = at("staged", [P, 2, TT, CW])
        prob = at("prob", [P, 2, TT, SEQ])
        probT = at("probT", [P, 2, 3 * P])
        bias = at("bias", [P, 2, TT, SEQ])
        level = at("level", [P, LEVELS, P], U8, 1)
        ropetmp = at("ropetmp", [P, TT, 4 * ROPE])
        aff = qkT[:, 0:4, :].rearrange("p (i k) s -> p i k s", i=2)
        osb = pre[:, :, :].rearrange("p h s -> p (h s)").rearrange("p (t c) -> p t c", t=TT)
        osq = suf[:, :, :].rearrange("p h s -> p (h s)").rearrange("p (t c) -> p t c", t=TT)
        heads = lambda m: m.rearrange("p t (h c) -> p (t h) c", c=HEAD)
        par_rows = prob[:, :, :, :].rearrange("p i t s -> p (i t s)")[:, 0:3 * P].rearrange(
            "p (a c) -> p a c", a=3)
        lb_rows = staged[:, 0, 0, 0:P]

        ps = ctx.enter_context(nc.psum_tensor("ps", [P, 8, CW], F32))

        raw_in = [sem(f"raw_in{s}") for s in range(RING)]
        hi_done, lo_done, pe_used = sem("hi_done"), sem("lo_done"), sem("pe_used")
        psum_full = [sem(f"psum_full{b}") for b in range(8)]
        psum_free = [sem(f"psum_free{b}") for b in range(8)]
        x_in, const_in, lb_in = sem("x_in"), sem("const_in"), sem("lb_in")
        masks_in, params_in, small_in = sem("masks_in"), sem("params_in"), sem("small_in")
        ln1_in, ln2_in = sem("ln1_in"), sem("ln2_in")
        unit_par = sem("unit_par")
        lb_turned, lb_max, lb_exp = sem("lb_turned"), sem("lb_max"), sem("lb_exp")
        xhi_done, x_ready, natural = sem("xhi_done"), sem("x_ready"), sem("natural")
        rope_done, f_ready, qk_ready = sem("rope_done"), sem("f_ready"), sem("qk_ready")
        max_done, exp_done, prob_done = sem("max_done"), sem("exp_done"), sem("prob_done")
        ovar_done, ostd_done, gate_done, o_gated = (sem("ovar_done"), sem("ostd_done"), sem("gate_done"),
                                                    sem("o_gated"))
        ln_var, ln_std, ln_done = sem("ln_var"), sem("ln_std"), sem("ln_done")
        half_done, conv_done, silu_done = sem("half_done"), sem("conv_done"), sem("silu_done")
        h_full, h_hi, h_done = sem("h_full"), sem("h_hi"), sem("h_done")
        act_link, dve_link, pool_link, ffn_link = (sem("act_link"), sem("dve_link"), sem("pool_link"),
                                                   sem("ffn_link"))
        taps_done = sem("taps_done")
        fin_done, out_done, first_rows = sem("fin_done"), sem("out_done"), sem("first_rows")

        CREDIT = RING

        def wait_full(eng, layer, bank, use):
            eng.wait_ge(psum_full[bank], layer * len(FULL[bank]) + (FULL[bank].index(use) + 1))

        def wait_free(pe, layer, bank, use):
            pe.wait_ge(psum_free[bank], layer * len(USES[bank]) + (USES[bank].index(use) + 1))

        def wait_read(eng, layer, bank, use):
            eng.wait_ge(psum_free[bank], layer * len(USES[bank]) + (USES[bank].index(use) + 2))

        def wait_groups(eng, layer, n):
            eng.wait_ge(pe_used, layer * GROUPS + (n + CREDIT))

        def carry_wait(eng, n):
            if eng is nc.vector:
                eng.memset(spare[:, n:n + 1], 0.0)
            else:
                eng.tensor_tensor(spare[:, n:n + 1], spare[:, 0:1], spare[:, 0:1], ALU.add)

        class Link:

            def __init__(self, eng, semaphore):
                self.eng, self.sem, self.base, self.n = eng, semaphore, 0, 0

            def __call__(self, ins):
                self.n += 1
                ins.then_inc(self.sem, 1)
                self.eng.wait_ge(self.sem, self.base + self.n)

        block = ctx.enter_context(nc.Block())

        @block.sync
        def _(sp):
            sp.dma_start(xres[:, :, :], x.rearrange("b (t p) d -> p (b t) d", p=P)).then_inc(x_in, 16)
            sp.dma_start(ident[:, :], c_ident[:, :]).then_inc(const_in, 16)
            sp.dma_start(rope[:, :, :, :], c_rope.rearrange("a (t p) r -> p a t r", p=P)).then_inc(const_in, 16)
            sp.dma_start(lb_rows[0:DEPTH * A_HEADS, :], lb_logits.rearrange("l (h k) -> (l h) k", k=P))\
                .then_inc(lb_in, 16)

            def load(w, layer, moving, n, row, col):
                s = n % RING
                sp.wait_ge(lo_done, layer * GROUPS + moving + (n + 1 - RING + CREDIT))
                if row == 0:
                    sp.sem_inc(first_rows, 1)
                src = w[bass.ds(layer, 1), row * P:(row + GK) * P, bass.ds(col, CW)]
                sp.dma_start(raw[:, s, :, :], src.rearrange("l (k p) n -> p (l k) n", p=P)).then_inc(raw_in[s], 16)

            with sp.Fori(0, DEPTH) as layer:
                for i, chunk in enumerate(ORDER[:2]):
                    for j in range(GC):
                        load(w_in, layer, 0, i * GC + j, j * GK, chunk * CW)
                with sp.Fori(4, NC_IN) as chunk:
                    for j in range(GC):
                        load(w_in, layer, chunk * GC, j - 2 * GC, j * GK, chunk * CW)
                for i in (I_AT, G_AT):
                    for j in range(GC):
                        load(w_in, layer, 0, i * GC + j, j * GK, ORDER[i] * CW)
                with sp.Fori(0, NC_OUT) as c:
                    for j in range(GC):
                        load(w_out, layer, c * GC, BASE_OUT + j, MIX_ORDER[j] * GK, c * CW)
                with sp.Fori(0, NC_FF) as c:
                    for half, w in enumerate((w_gate, w_up)):
                        for j in range(GC):
                            load(w, layer, c * (2 * GC), BASE_FFN + half * GC + j, j * GK, c * CW)
                with sp.Fori(0, NC_OUT // 2) as two:
                    for half in range(2):
                        col = sp.snap(two * (2 * CW) + half * CW)
                        for j in range(GD):
                            load(w_down, layer, two * (2 * GD), BASE_DOWN + half * GD + j, j * GK, col)
            for t in range(TT):
                sp.wait_ge(fin_done, t + 1)
                sp.dma_start(out.rearrange("b (t p) d -> (b t) p d", p=P)[t], xres[:, t, :]).then_inc(out_done, 16)
            sp.wait_ge(out_done, 16 * TT)

        @block.gpsimd
        def _(pool):
            link = Link(pool, pool_link)
            pool.memset(spare[:, 0:1], 0.0)
            pool.memset(sinks[:, 0:B_HEADS], NEG)
            pool.memset(parT[:, PAR_LN[0]:PAR_LN[0] + KT], 1.0)
            pool.memset(parT[:, PAR_LN[0] + KT:PAR_LN[0] + 2 * KT], 0.0).then_inc(unit_par, 1)
            pool.wait_ge(unit_par, 1)
            for a in range(2):
                pool.dma_start(lnb[:, a, :], c_unit[a:a + 1, :].broadcast_to([P, D_MODEL])).then_inc(ln2_in, 16)

            def row(a, layer):
                return a[bass.ds(layer, 1), :]

            def natural_affine(layer, which):
                for b in range(8):
                    wait_full(pool, layer, b, ("xturn", which))
                pool.wait_ge((ln2_in, ln1_in)[which], layer * 32 + 32)
                for t in range(TT):
                    link(pool.tensor_tensor(xres[:, t, :], xres[:, t, :], lnb[:, 0, :], ALU.mult))
                    pool.tensor_tensor(xres[:, t, :], xres[:, t, :], lnb[:, 1, :], ALU.add).then_inc(natural, 1)

            with pool.Fori(0, DEPTH) as layer:
                link.base, link.n = layer * POOL_LINKS, 0
                wait_groups(pool, layer, 0)
                carry_wait(pool, 1)
                pool.dma_start(bias[:, :, :, :], c_bias.rearrange("a (t p) s -> p a t s", p=P)).then_inc(masks_in, 16)
                pool.dma_start(att[:, :, :], c_level.rearrange("n p s -> p n s")).then_inc(masks_in, 16)
                for n, a in enumerate((ln1_g, ln1_b, ln2_g, ln2_b)):
                    pool.dma_start(par_rows[n * KT:(n + 1) * KT, 0, :],
                                   row(a, layer).rearrange("l (k p) -> (l k) p", p=P)).then_inc(params_in, 16)
                for (r, n), a in zip(((4 * KT, 0), (0, 1), (FT, 1), (0, 2)),
                                     [conv_w[bass.ds(layer, 1), j, :] for j in range(TAPS)] + [row(conv_b, layer)]):
                    pool.dma_start(par_rows[r:r + FT, n, :], a.rearrange("l (k p) -> (l k) p", p=P))\
                        .then_inc(params_in, 16)
                pool.dma_start(anorm[:, :], row(a_norm_w, layer).broadcast_to([P, HEAD])).then_inc(small_in, 16)
                pool.dma_start(sinks[:, B_HEADS:N_HEADS], row(c_sinks, layer).broadcast_to([P, C_HEADS]))\
                    .then_inc(small_in, 16)
                natural_affine(layer, 0)
                pool.memset(suf[:, :, :], 1.0)
                pool.memset(ql[:, :, :], 0.0)
                link(pool.memset(kl[:, :, :], 0.0))

                for p in range(BASE_FFN):
                    for step, k in STEPS.get(p, ()):
                        if step == "evac" and rope_blocks(ORDER[k]):
                            if k == ROPES[0]:
                                pool.wait_ge(const_in, 32)
                            wait_read(pool, layer, in_banks(k)[1], ("proj", k))
                            b0, nb = rope_blocks(ORDER[k])[0], len(rope_blocks(ORDER[k]))
                            half = ROPE // 2
                            if k != ROPES[0]:
                                pool.wait_ge(rope_done, layer * (TT * len(ROPES)) + TT * ROPES.index(k))
                            for t in range(TT):
                                v = staged[:, k % 2, t, b0 * P:(b0 + nb) * P].rearrange("p (b c) -> p b c", c=P)
                                tmp = ropetmp[:, t, 0:nb * ROPE].rearrange("p (b c) -> p b c", c=ROPE)
                                cos, sin = (rope[:, a, t, :].unsqueeze(1).broadcast_to([P, nb, ROPE])
                                            for a in (0, 1))
                                pool.tensor_tensor(tmp[:, :, 0:half], v[:, :, half:ROPE], sin[:, :, 0:half],
                                                   ALU.mult)
                                link(pool.tensor_tensor(tmp[:, :, half:ROPE], v[:, :, 0:half],
                                                        sin[:, :, half:ROPE], ALU.mult))
                                link(pool.tensor_tensor(v[:, :, 0:ROPE], v[:, :, 0:ROPE], cos, ALU.mult))
                                pool.tensor_tensor(v[:, :, 0:ROPE], v[:, :, 0:ROPE], tmp, ALU.add)\
                                    .then_inc(rope_done, 1)
                        if step == "level" and k >= 1:
                            h = 2 ** (k - 1)
                            if k == 1:
                                pool.wait_ge(f_ready, layer + 1)
                                wait_read(pool, layer, 5, ("turn", 1))
                            else:
                                wait_full(pool, layer, 7, ("level", k - 1))
                            first, second = (lambda m, a=a: m[:, :, :].rearrange(
                                "p a (n two h) -> p (a n) two h", two=2, h=h)[:, :, a, :] for a in (0, 1))
                            pool.tensor_tensor(second(ql), second(qT), second(pre), ALU.mult)
                            pool.tensor_tensor(first(kl), first(kT), first(suf), ALU.mult).then_inc(qk_ready, 1)
                            if k < LEVELS:
                                pool.wait_ge(qk_ready, layer * LEVELS + k)
                                shape = [P, A_HEADS * SEQ // (2 * h), h]
                                link(pool.tensor_tensor(first(suf), first(suf),
                                                        second(pre)[:, :, h - 1:h].broadcast_to(shape), ALU.mult))
                                link(pool.tensor_tensor(second(pre), second(pre),
                                                        first(pre)[:, :, h - 1:h].broadcast_to(shape), ALU.mult))
                        if step == "evac" and k == G_AT:
                            wait_read(pool, layer, in_banks(k)[1], ("proj", k))
                            pool.wait_ge(small_in, layer * 32 + 32)
                            pool.tensor_tensor(heads(gA[:, :, :]), heads(gA[:, :, :]), anorm[:, :].unsqueeze(1).broadcast_to(
                                [P, TT * A_HEADS, HEAD]), ALU.mult).then_inc(gate_done, 1)
                pool.wait_ge(x_ready, layer * 24 + 16)
                carry_wait(pool, 2)
                pool.dma_start(lnb[:, 0, :], row(ln1_g, layer).broadcast_to([P, D_MODEL])).then_inc(ln1_in, 16)
                pool.dma_start(lnb[:, 1, :], row(ln1_b, layer).broadcast_to([P, D_MODEL])).then_inc(ln1_in, 16)
                natural_affine(layer, 1)
                pool.wait_ge(h_done, layer * PAIRS + PAIRS)
                carry_wait(pool, 3)
                pool.dma_start(lnb[:, 0, :], row(ln2_g, layer).broadcast_to([P, D_MODEL])).then_inc(ln2_in, 16)
                pool.dma_start(lnb[:, 1, :], row(ln2_b, layer).broadcast_to([P, D_MODEL])).then_inc(ln2_in, 16)
            assert link.n == POOL_LINKS, link.n

        @block.scalar
        def _(act):
            link = Link(act, act_link)
            act.wait_ge(lb_max, 1)
            act.activation(lbw[:, 1, :, :], lbw[:, 0, :, :], ACT.Exp).then_inc(lb_exp, 1)

            def split_hi(layer, moving, n):
                s = n % RING
                act.wait_ge(raw_in[s], layer * (LAYER_FILLS * 16) + fills(moving) + (n // RING + 1) * 16)
                wait_groups(act, layer, moving + (n + 1 - RING))
                act.activation(whi[:, s, :, :], raw[:, s, :, :], ACT.Copy).then_inc(hi_done, 1)

            def fills(moving):
                return moving * (16 // RING)

            def x_hi(layer, which, b):
                number = layer * 24 + 16 * which + b
                if b % 2 == 0:
                    wait_full(act, layer, b, ("xturn", which))
                    if which == 0 and b == 0:
                        act.wait_ge(unit_par, 1)
                    if b >= 2:
                        act.wait_ge(x_ready, number - 1)
                    for kk in range(2):
                        col = PAR_LN[which] + 2 * b + kk
                        ins = act.activation(aff[:, 0, kk, :], ps[:, b, kk * SEQ:(kk + 1) * SEQ], ACT.Identity,
                                             scale=parT[:, col:col + 1], bias=parT[:, col + KT:col + KT + 1])
                    ins.then_inc(psum_free[b], 1)
                wait_read(act, layer, b, ("xturn", which))
                act.activation(xT[:, 2 * b:2 * b + 2, 0, :], aff[:, b % 2, :, :], ACT.Copy).then_inc(xhi_done, 1)

            def root(layer, which):
                act.wait_ge(ln_var, layer * 2 + (which + 1))
                act.activation(lns[:, 1, :], lns[:, 0, :], ACT.Sqrt).then_inc(ln_std, 1)

            def low_sum(layer, c, half, q):
                wait_groups(act, layer, c * (2 * GC) + (BASE_FFN + (half + 1) * GC))
                if half == 0:
                    act.wait_ge(natural, layer * 4 + 4)
                b = 4 * half + 2 * q
                act.activation(fsum[:, q, :, :], ps[:, b:b + 2, SEQ:2 * SEQ], ACT.Copy).then_inc(half_done, 1)

            def silu(layer, c, q):
                act.wait_ge(conv_done, layer * PAIRS + c * 2 + (q + 1))
                act.activation(fsilu[:, q, :, :], fconv[:, q, :, :], ACT.Silu).then_inc(silu_done, 1)

            def hidden_hi(layer, c, q):
                act.wait_ge(h_full, layer * PAIRS + c * 2 + (q + 1))
                act.activation(hT[:, bass.ds(c * 4 + 2 * q, 2), 0, :], fconv[:, q, :, :], ACT.Copy)\
                    .then_inc(h_hi, 1)

            def ffn_chunk(layer, c, first):
                for j in range(GC):
                    if first:
                        x_hi(layer, 1, j)
                    split_hi(layer, c * (2 * GC), BASE_FFN + j)
                    if not first:
                        if j in (3, 5):
                            low_sum(layer, c - 1, 1, (j - 3) // 2)
                        if j in (4, 6):
                            hidden_hi(layer, c - 1, (j - 4) // 2)
                for j in range(GC):
                    split_hi(layer, c * (2 * GC), BASE_FFN + GC + j)
                    if j in (3, 5):
                        low_sum(layer, c, 0, (j - 3) // 2)
                    if j in (4, 6):
                        silu(layer, c, (j - 4) // 2)

            with act.Fori(0, DEPTH) as layer:
                link.base, link.n = layer * ACT_LINKS, 0
                for p in range(BASE_FFN + LAG):
                    if p < 8:
                        x_hi(layer, 0, p)
                    if p < BASE_FFN:
                        split_hi(layer, 0, p)
                    for step, k in STEPS.get(p - LAG, ()):
                        if step == "evac":
                            chunk = ORDER[k]
                            wait_groups(act, layer, GC * (k + 1))
                            for t in range(TT):
                                src = ps[:, in_banks(k)[t], :]
                                if chunk == I_CHUNK:
                                    last = act.activation(iA[:, t, :], src, ACT.Copy)
                                elif chunk == G_CHUNK:
                                    last = act.activation(gA[:, t, :], src, ACT.Silu)
                                else:
                                    for dst, b0, b1 in parts(chunk):
                                        c0 = 4 * chunk
                                        src_cols = slice((b0 - c0) * P, (b1 - c0) * P)
                                        if dst == "vB":
                                            to = vB[:, t, (b0 - VB0) * P:(b1 - VB0) * P]
                                        elif dst == "vC":
                                            to = vC[:, t, (b0 - VC0) * P:(b1 - VC0) * P]
                                        else:
                                            to = staged[:, k % 2, t, src_cols]
                                        last = act.activation(to, src[:, src_cols], ACT.Copy)
                                last.then_inc(psum_free[in_banks(k)[t]], 1)
                        if step == "turn":
                            for pair in turned_pairs(ORDER[k]):
                                wait_full(act, layer, 4 + pair, (step, k))
                                src = ps[:, 4 + pair, :].rearrange("p (b s) -> p b s", b=2)
                                if ORDER[k] == F_CHUNK:
                                    ins = act.activation(pre[:, 2 * pair:2 * pair + 2, :], src, ACT.Sigmoid)
                                elif ORDER[k] == Q_CHUNK:
                                    ins = act.activation(qT[:, 2 * pair:2 * pair + 2, :], src, ACT.Silu)
                                else:
                                    slot = qk_slot(4 * ORDER[k] + 2 * pair)
                                    ins = act.activation(qkT[:, slot:slot + 2, :], src, ACT.Copy)
                                ins.then_inc(psum_free[4 + pair], 1)
                        if step == "score":
                            act.wait_ge(max_done, layer * N_HEADS + (k + 1))
                            i = k % 2
                            for t in range(TT):
                                keys = (t + 1) * P
                                act.activation(prob[:, i, t, 0:keys], prob[:, i, t, 0:keys], ACT.Exp,
                                               bias=hd[:, i, 1, t:t + 1], accum_out=hd[:, i, 2, t:t + 1])
                            act.activation(hd[:, i, 3, :], hd[:, i, 1, :], ACT.Exp, bias=sinks[:, k:k + 1])\
                                .then_inc(exp_done, 1)
                        if step == "value":
                            wait_full(act, layer, 5, (step, k))
                            if k == 0:
                                act.wait_ge(natural, layer * 4 + 2)
                            act.activation(mix[:, A_HEADS + k, :], ps[:, 5, 0:SEQ], ACT.Copy)\
                                .then_inc(psum_free[5], 1)
                        if step == "hout":
                            for t in range(TT):
                                wait_full(act, layer, 6 + t, (step, k))
                                act.activation(osb[:, t, :], ps[:, 6 + t, :], ACT.Copy).then_inc(psum_free[6 + t], 1)
                        if step == "hsquare":
                            act.wait_ge(ovar_done, layer + 1)
                            act.activation(hs[:, 2, :], hs[:, 1, :], ACT.Sqrt).then_inc(ostd_done, 1)
                        if step == "hturn":
                            for pair in range(2):
                                wait_full(act, layer, 4 + pair, (step, k))
                                act.activation(mix[:, 2 * pair:2 * pair + 2, :],
                                               ps[:, 4 + pair, :].rearrange("p (b s) -> p b s", b=2), ACT.Copy)\
                                    .then_inc(psum_free[4 + pair], 1)
                        if step == "mixsplit":
                            b = MIX_ORDER[k]
                            if k == 0:
                                wait_groups(act, layer, BASE_OUT)
                            if b < 2:
                                wait_read(act, layer, 4 + b, ("hturn", 0))
                            else:
                                wait_read(act, layer, 5, ("value", 2 * b + 1 - A_HEADS))
                            act.activation(xT[:, 2 * b:2 * b + 2, 0, :], mix[:, 2 * b:2 * b + 2, :], ACT.Copy)\
                                .then_inc(xhi_done, 1)
                root(layer, 0)
                ffn_chunk(layer, 0, True)
                with act.Fori(1, NC_FF) as c:
                    ffn_chunk(layer, c, False)
                for n in range(NC_OUT * GD):
                    split_hi(layer, 0, BASE_DOWN + n)
                    if n in (3, 5):
                        low_sum(layer, NC_FF - 1, 1, (n - 3) // 2)
                    if n in (4, 6):
                        hidden_hi(layer, NC_FF - 1, (n - 4) // 2)
                root(layer, 1)

        @block.vector
        def _(dve):
            link = Link(dve, dve_link)
            for b in range(7):
                dve.nop().then_inc(psum_free[b], 1)
            dve.nop().then_inc(lo_done, CREDIT)
            dve.nop().then_inc(ln_done, CREDIT)
            dve.wait_ge(lb_turned, 1)
            logits, e, t0, cum, low, rest = (lbw[:, a, :, :] for a in range(6))
            dve.tensor_copy(logits, ps[:, 7, 0:DEPTH * A_HEADS].rearrange("p (l h) -> p l h", l=DEPTH))\
                .then_inc(psum_free[7], 1)
            dve.wait_ge(psum_free[7], 1)
            link(dve.reduce_max(t0[:, 0, :], logits.rearrange("p l h -> p h l"), AX.X))
            dve.tensor_tensor(logits, logits, t0[:, 0:1, :].broadcast_to([P, DEPTH, A_HEADS]), ALU.subtract)\
                .then_inc(lb_max, 1)
            dve.wait_ge(lb_exp, 1)
            link(dve.reduce_sum(t0[:, 0, :], e.rearrange("p l h -> p h l"), AX.X))
            link(dve.reciprocal(t0[:, 1, :], t0[:, 0, :]))
            link(dve.tensor_tensor(e, e, t0[:, 1:2, :].broadcast_to([P, DEPTH, A_HEADS]), ALU.mult))
            link(dve.tensor_copy(cum[:, 0, :], e[:, 0, :]))
            for n in range(1, DEPTH):
                link(dve.tensor_tensor(cum[:, n, :], cum[:, n - 1, :], e[:, n, :], ALU.add))
            link(dve.tensor_tensor(low, cum, cum[:, 0:1, :].broadcast_to([P, DEPTH, A_HEADS]), ALU.subtract))
            link(dve.tensor_scalar(rest, low, -1.0, 1.0, ALU.mult, ALU.add))
            before = link.n

            def split_lo(layer, moving, n):
                s = n % RING
                dve.wait_ge(hi_done, layer * GROUPS + moving + (n + 1))
                dve.tensor_tensor(wlo[:, s, :, :], raw[:, s, :, :], whi[:, s, :, :].bitcast(F32), ALU.subtract)\
                    .then_inc(lo_done, 1)

            def x_lo(layer, which, b):
                if b % 2 == 1:
                    wait_full(dve, layer, b, ("xturn", which))
                    if b >= 3:
                        dve.wait_ge(x_ready, layer * 24 + (16 * which + b - 1))
                    for kk in range(2):
                        col = PAR_LN[which] + 2 * b + kk
                        ins = dve.tensor_scalar(aff[:, 1, kk, :], ps[:, b, kk * SEQ:(kk + 1) * SEQ],
                                                parT[:, col:col + 1], parT[:, col + KT:col + KT + 1],
                                                ALU.mult, ALU.add)
                    ins.then_inc(psum_free[b], 1)
                low_part(layer, 16 * which + b, 2 * b, aff[:, b % 2, :, :])

            def low_part(layer, n, kt, whole):
                dve.wait_ge(xhi_done, layer * 24 + (n + 1))
                dve.tensor_tensor(xT[:, kt:kt + 2, 1, :], whole, xT[:, kt:kt + 2, 0, :].bitcast(F32),
                                  ALU.subtract).then_inc(x_ready, 1)

            def y_chunk(layer, which, c, banks):
                use = ("out", "down")[which]
                wait_groups(dve, layer, BASE_OUT + GC * (c + 1) if which == 0 else BASE_DOWN + GD * (c + 1))
                if c == 0:
                    dve.wait_ge(natural, layer * 4 + 2 * (which + 1))
                cols = slice(c * CW, (c + 1) * CW)
                for t in range(TT):
                    dve.scalar_tensor_tensor(xres[:, t, cols], xres[:, t, cols], ALPHA, ps[:, banks[t], :],
                                             ALU.mult, ALU.add).then_inc(psum_free[banks[t]], 1)
                for t in range(TT):
                    wait_read(dve, layer, banks[t], (use, c))
                    last = dve.bn_stats(stats[:, t, c, :], xres[:, t, cols])
                link(last)

            def norm(layer, which):
                carry_wait(dve, 4 + which)
                for t in range(TT):
                    last = dve.bn_aggr(mv[:, t, :], stats[:, t, :, :].rearrange("p c s -> p (c s)"))
                link(last)
                dve.tensor_scalar(lns[:, 0, :], mv[:, :, 1], EPS, None, ALU.add).then_inc(ln_var, 1)
                dve.wait_ge(ln_std, layer * 2 + (which + 1))
                link(dve.reciprocal(lns[:, 2, :], lns[:, 1, :]))
                for half in range(2):
                    cols = slice(half * D_MODEL // 2, (half + 1) * D_MODEL // 2)
                    for t in range(TT):
                        dve.tensor_scalar(xres[:, t, cols], xres[:, t, cols], mv[:, t, 0:1], lns[:, 2, t:t + 1],
                                          ALU.subtract, ALU.mult).then_inc(ln_done, 1)

            def own(layer, c, n):
                dve.wait_ge(ffn_link, layer * FFN_LINKS + c * 8 + n)

            def gate(layer, c, q):
                dve.wait_ge(half_done, layer * (2 * PAIRS) + c * 4 + (q + 1))
                b = 2 * q
                g, y = fsum[:, q, :, :], fconv[:, q, :, :]
                dve.tensor_tensor(g, ps[:, b:b + 2, 0:SEQ], g, ALU.add).then_inc(ffn_link, 1)
                own(layer, c, 3 * q + 1)
                tap = lambda j, m: parC[:, j, 2 * q + m:2 * q + m + 1]
                for m in range(2):
                    ins = dve.tensor_scalar(y[:, m, :], g[:, m, :], tap(TAPS - 1, m), tap(TAPS, m),
                                            ALU.mult, ALU.add)
                ins.then_inc(ffn_link, 1)
                own(layer, c, 3 * q + 2)
                for m in range(2):
                    ins = dve.scalar_tensor_tensor(y[:, m, 1:], g[:, m, 0:SEQ - 1], tap(1, m), y[:, m, 1:],
                                                   ALU.mult, ALU.add)
                ins.then_inc(ffn_link, 1)
                own(layer, c, 3 * q + 3)
                for m in range(2):
                    ins = dve.scalar_tensor_tensor(y[:, m, 2:], g[:, m, 0:SEQ - 2], tap(0, m), y[:, m, 2:],
                                                   ALU.mult, ALU.add)
                ins.then_inc(conv_done, 1)

            def up(layer, c, q):
                dve.wait_ge(half_done, layer * (2 * PAIRS) + c * 4 + (q + 3))
                b = 4 + 2 * q
                u = fsum[:, q, :, :]
                dve.tensor_tensor(u, ps[:, b:b + 2, 0:SEQ], u, ALU.add).then_inc(ffn_link, 1)
                own(layer, c, 7 + q)
                dve.wait_ge(silu_done, layer * PAIRS + c * 2 + (q + 1))
                dve.tensor_tensor(fconv[:, q, :, :], u, fsilu[:, q, :, :], ALU.mult).then_inc(h_full, 1)

            def hidden_lo(layer, c, q):
                dve.wait_ge(h_hi, layer * PAIRS + c * 2 + (q + 1))
                tiles = bass.ds(c * 4 + 2 * q, 2)
                dve.tensor_tensor(hT[:, tiles, 1, :], fconv[:, q, :, :], hT[:, tiles, 0, :].bitcast(F32),
                                  ALU.subtract).then_inc(h_done, 1)

            def ffn_chunk(layer, c, first):
                for j in range(GC):
                    if first:
                        x_lo(layer, 1, j)
                    split_lo(layer, c * (2 * GC), BASE_FFN + j)
                    if not first:
                        if j in (3, 5):
                            up(layer, c - 1, (j - 3) // 2)
                        if j in (5, 7):
                            hidden_lo(layer, c - 1, (j - 5) // 2)
                if not first:
                    dve.wait_ge(conv_done, layer * PAIRS + c * 2)
                dve.tensor_copy(parC[:, :, :], conv[:, :, bass.ds(c * 4, 4)]).then_inc(taps_done, 1)
                for j in range(GC):
                    split_lo(layer, c * (2 * GC), BASE_FFN + GC + j)
                    if j == 3:
                        dve.wait_ge(taps_done, layer * NC_FF + c + 1)
                        if not first:
                            dve.wait_ge(h_done, layer * PAIRS + c * 2)
                    if j in (3, 5):
                        gate(layer, c, (j - 3) // 2)

            with dve.Fori(0, DEPTH) as layer:
                link.base, link.n = layer * DVE_LINKS + before, 0
                for p in range(BASE_FFN + LAG):
                    if p < 8:
                        x_lo(layer, 0, p)
                    if p < BASE_FFN:
                        split_lo(layer, 0, p)
                    for step, k in STEPS.get(p - LAG, ()):
                        if step == "params":
                            dve.wait_ge(masks_in, layer * 32 + 32)
                            dve.tensor_copy(level[:, :, :], att[:, :, :])
                            wait_full(dve, layer, 6, (step, k))
                            dve.tensor_copy(parT[:, :], ps[:, 6, 0:PAR_COLS]).then_inc(psum_free[6], 1)
                        if step == "turn" and ORDER[k] == F_CHUNK:
                            link(dve.tensor_copy(lbc[:, :, :, :], lbw[:, 4:6, bass.ds(layer, 1), :]))
                            wait_read(dve, layer, 5, (step, k))
                            for h in range(A_HEADS):
                                last = dve.tensor_scalar(pre[:, h, :], pre[:, h, :], lbc[:, 1, 0, h:h + 1],
                                                         lbc[:, 0, 0, h:h + 1], ALU.mult, ALU.add)
                            link(last)
                            dve.tensor_scalar(kT[:, :, :], pre[:, :, :], -1.0, 1.0, ALU.mult, ALU.add)\
                                .then_inc(f_ready, 1)
                            link(dve.memset(att[:, :, :], 0.0))
                        if step == "level" and k < LEVELS:
                            for b in (6, 7):
                                wait_full(dve, layer, b, (step, k))
                                carry_wait(dve, 6 + 2 * k + b % 2)
                                dve.copy_predicated(
                                    att[:, 4 * (b - 6):4 * (b - 5), :],
                                    level[:, k, :].unsqueeze(1).broadcast_to([P, 4, P]),
                                    ps[:, b, :].rearrange("p (a s) -> p a s", s=P)).then_inc(psum_free[b], 1)
                        if step == "level" and k == LEVELS:
                            wait_full(dve, layer, 6, (step, k))
                            dve.tensor_copy(att01[:, :, :], ps[:, 6, :].rearrange("p (a s) -> p a s", s=P))\
                                .then_inc(psum_free[6], 1)
                        if step == "score":
                            i, bank = k % 2, 6 + k % 2
                            wait_full(dve, layer, bank, (step, k))
                            if k == 0:
                                dve.wait_ge(small_in, layer * 32 + 32)
                            dve.scalar_tensor_tensor(prob[:, i, :, :].rearrange("p t s -> p (t s)"), ps[:, bank, :],
                                                     SCALE, bias[:, int(k >= B_HEADS), :, :].rearrange(
                                                         "p t s -> p (t s)"), ALU.mult, ALU.add)\
                                .then_inc(psum_free[bank], 1)
                            wait_read(dve, layer, bank, (step, k))
                            link(dve.reduce_max(hd[:, i, 0, :], prob[:, i, :, :], AX.X))
                            dve.tensor_scalar(hd[:, i, 1, :], hd[:, i, 0, :], sinks[:, k:k + 1], -1.0, ALU.max,
                                              ALU.mult).then_inc(max_done, 1)
                        if step == "finish":
                            i = k % 2
                            dve.wait_ge(exp_done, layer * N_HEADS + (k + 1))
                            link(dve.tensor_tensor(hd[:, i, 2, :], hd[:, i, 2, :], hd[:, i, 3, :], ALU.add))
                            link(dve.reciprocal(hd[:, i, 4, :], hd[:, i, 2, :]))
                            for t in range(TT):
                                keys = (t + 1) * P
                                last = dve.tensor_scalar(prob[:, i, t, 0:keys], prob[:, i, t, 0:keys],
                                                         hd[:, i, 4, t:t + 1], None, ALU.mult)
                            last.then_inc(prob_done, 1)
                        if step == "flip":
                            wait_full(dve, layer, 4, (step, k))
                            dve.tensor_copy(probT[:, k % 2, :], ps[:, 4, 0:3 * P]).then_inc(psum_free[4], 1)
                        if step == "hsquare":
                            wait_read(dve, layer, 7, ("hout", 0))
                            link(dve.tensor_tensor(osq, osb, osb, ALU.mult))
                            link(dve.reduce_sum(hs[:, 0, :], heads(osq), AX.X))
                            dve.tensor_scalar(hs[:, 1, :], hs[:, 0, :], 1.0 / HEAD, EPS, ALU.mult, ALU.add)\
                                .then_inc(ovar_done, 1)
                        if step == "hscale":
                            dve.wait_ge(ostd_done, layer + 1)
                            link(dve.reciprocal(hs[:, 3, :], hs[:, 2, :]))
                            link(dve.tensor_tensor(heads(osb), heads(osb), hs[:, 3, :].unsqueeze(2).broadcast_to(
                                [P, TT * A_HEADS, HEAD]), ALU.mult))
                        if step == "hgate":
                            dve.wait_ge(gate_done, layer + 1)
                            dve.tensor_tensor(osb, osb, gA[:, :, :], ALU.mult).then_inc(o_gated, 1)
                        if step == "mixsplit":
                            b = MIX_ORDER[k]
                            low_part(layer, 8 + k, 2 * b, mix[:, 2 * b:2 * b + 2, :])
                        if step == "yevac":
                            y_chunk(layer, 0, k, out_banks(k))
                norm(layer, 0)
                ffn_chunk(layer, 0, True)
                with dve.Fori(1, NC_FF) as c:
                    ffn_chunk(layer, c, False)
                for n in range(NC_OUT * GD):
                    split_lo(layer, 0, BASE_DOWN + n)
                    if n in (3, 5):
                        up(layer, NC_FF - 1, (n - 3) // 2)
                    if n in (5, 7):
                        hidden_lo(layer, NC_FF - 1, (n - 5) // 2)
                    if n >= GD and n % GD == LAG - 1:
                        y_chunk(layer, 1, n // GD - 1, in_banks(n // GD - 1))
                y_chunk(layer, 1, NC_OUT - 1, in_banks(NC_OUT - 1))
                norm(layer, 1)
            assert link.n == DVE_LINKS, link.n
            link.base = before + DEPTH * DVE_LINKS - link.n
            dve.wait_ge(ln2_in, 32 * (DEPTH + 1))
            dve.wait_ge(ln_done, CREDIT + 8 * DEPTH)
            for t in range(TT):
                link(dve.tensor_tensor(xres[:, t, :], xres[:, t, :], lnb[:, 0, :], ALU.mult))
                dve.tensor_tensor(xres[:, t, :], xres[:, t, :], lnb[:, 1, :], ALU.add).then_inc(fin_done, 1)

        @block.tensor
        def _(pe):
            pe.nop().then_inc(pe_used, CREDIT)
            pe.wait_ge(const_in, 32)
            pe.wait_ge(lb_in, 16)
            rows = DEPTH * A_HEADS
            pe.transpose(ps[:, 7, 0:rows], lb_rows[0:rows, :], ident[0:rows, 0:rows]).then_inc(lb_turned, 1)
            pe.wait_ge(x_in, 16)

            def turn_x(layer, which):
                for b in range(8):
                    wait_free(pe, layer, b, ("xturn", which))
                    pe.wait_ge(ln_done, layer * 8 + (4 * which - 4 + 2 * (b // 4 + 1) + CREDIT))
                    for kk in range(2):
                        for t in range(TT):
                            ins = pe.transpose(ps[:, b, kk * SEQ + t * P:kk * SEQ + (t + 1) * P],
                                               xres[:, t, (2 * b + kk) * P:(2 * b + kk + 1) * P], ident[:, :])
                    ins.then_inc(psum_full[b], 1)

            def rows_times_chunk(layer, n, stationary, kts, banks, first, last):
                s = n % RING
                pe.wait_ge(lo_done, layer * GROUPS + (n + 1 + CREDIT))
                for t in range(TT):
                    toks = slice(t * P, (t + 1) * P)
                    for kk, kt in enumerate(kts):
                        hi, lo = stationary[:, kt, 0, toks], stationary[:, kt, 1, toks]
                        pe.matmul(ps[:, banks[t], :], hi, whi[:, s, kk, :], start=first and kk == 0, stop=False)
                        pe.matmul(ps[:, banks[t], :], hi, wlo[:, s, kk, :], start=False, stop=False)
                        ins = pe.matmul(ps[:, banks[t], :], lo, whi[:, s, kk, :], start=False,
                                        stop=last and kk == GK - 1)
                ins.then_inc(pe_used, 1)

            def ffn_chunk(layer, c, first):
                for half in range(2):
                    for j in range(GC):
                        s = j % RING
                        if first and half == 0:
                            pe.wait_ge(x_ready, layer * 24 + (17 + j))
                        if j == 0 and first:
                            for b in range(4 * half, 4 * half + 4):
                                wait_read(pe, layer, b, ("xturn", 1))
                        if j == 0 and not first:
                            pe.wait_ge((conv_done, h_full)[half], layer * PAIRS + c * 2)
                        pe.wait_ge(lo_done, layer * GROUPS + c * (2 * GC) + (BASE_FFN + half * GC + j + 1 + CREDIT))
                        for kk in range(GK):
                            kt = GK * j + kk
                            for m in range(4):
                                cols = slice(m * P, (m + 1) * P)
                                bank = 4 * half + m
                                for part in ((whi, wlo) if kt < KT - 1 else (wlo, whi)):
                                    if part is whi:
                                        ins = pe.matmul(ps[:, bank, :], whi[:, s, kk, cols],
                                                        xT[:, kt, :, :].rearrange("p a s -> p (a s)"),
                                                        start=kt == 0, stop=kt == KT - 1)
                                    else:
                                        ins = pe.matmul(ps[:, bank, 0:SEQ], wlo[:, s, kk, cols], xT[:, kt, 0, :],
                                                        start=False, stop=False, skip_group_check=True)
                        ins.then_inc(pe_used, 1)

            with pe.Fori(0, DEPTH) as layer:
                turn_x(layer, 0)
                for p in range(BASE_FFN):
                    i, j = p // GC, p % GC
                    if p < BASE_OUT:
                        banks, kts = in_banks(i), (GK * j, GK * j + 1)
                        if i == 0:
                            pe.wait_ge(x_ready, layer * 24 + (j + 1))
                        if j == 0:
                            for b in banks:
                                wait_free(pe, layer, b, ("proj", i))
                    else:
                        c = i - NC_IN
                        banks, kts = out_banks(c), (GK * MIX_ORDER[j], GK * MIX_ORDER[j] + 1)
                        if c == 0:
                            pe.wait_ge(x_ready, layer * 24 + (9 + j))
                        if j == 0:
                            for b in banks:
                                wait_free(pe, layer, b, ("out", c))
                    rows_times_chunk(layer, p, xT, kts, banks, j == 0, j == GC - 1)
                    for step, k in STEPS.get(p, ()):
                        if step == "params":
                            pe.wait_ge(params_in, layer * 128 + 128)
                            wait_free(pe, layer, 6, (step, k))
                            col = 0
                            for n, rows in enumerate(PAR_SETS):
                                ins = pe.transpose(ps[:, 6, col:col + rows], par_rows[0:rows, n, :],
                                                   ident[0:rows, 0:rows])
                                col += rows
                            ins.then_inc(psum_full[6], 1)
                        if step == "turn":
                            if ORDER[k] in (F_CHUNK, Q_CHUNK):
                                wait_read(pe, layer, in_banks(k)[1], ("proj", k))
                            else:
                                pe.wait_ge(rope_done, layer * (TT * len(ROPES)) + TT * (ROPES.index(k) + 1))
                            for pair in turned_pairs(ORDER[k]):
                                wait_free(pe, layer, 4 + pair, (step, k))
                                for b in range(2):
                                    for t in range(TT):
                                        c0 = (2 * pair + b) * P
                                        ins = pe.transpose(
                                            ps[:, 4 + pair, b * SEQ + t * P:b * SEQ + (t + 1) * P],
                                            staged[:, k % 2, t, c0:c0 + P], ident[:, :])
                                ins.then_inc(psum_full[4 + pair], 1)
                        if step == "level" and k < LEVELS:
                            q, key = (qT, kT) if k == 0 else (ql, kl)
                            if k == 0:
                                pe.wait_ge(f_ready, layer + 1)
                                wait_read(pe, layer, 5, ("turn", 1))
                            else:
                                pe.wait_ge(qk_ready, layer * LEVELS + k)
                            for b in (6, 7):
                                wait_free(pe, layer, b, (step, k))
                                for a in range(4):
                                    h, t = divmod(4 * (b - 6) + a, TT)
                                    toks = slice(t * P, (t + 1) * P)
                                    ins = pe.matmul(ps[:, b, a * P:(a + 1) * P], key[:, h, toks], q[:, h, toks],
                                                    start=True, stop=True)
                                ins.then_inc(psum_full[b], 1)
                        if step == "level" and k == LEVELS:
                            pe.wait_ge(qk_ready, layer * LEVELS + k)
                            wait_free(pe, layer, 6, (step, k))
                            for h in range(A_HEADS):
                                ins = pe.matmul(ps[:, 6, h * P:(h + 1) * P], kl[:, h, 0:P], ql[:, h, P:SEQ],
                                                start=True, stop=True)
                            ins.then_inc(psum_full[6], 1)
                        if step == "score":
                            bank = 6 + k % 2
                            if k in (0, B_HEADS):
                                wait_read(pe, layer, *((5, ("turn", B_TURN)) if k == 0 else (4, ("turn", C_TURN))))
                            wait_free(pe, layer, bank, (step, k))
                            if k < B_HEADS:
                                q, key = k, B_HEADS + k
                            else:
                                q = B_HEADS + k
                                key = 2 * B_HEADS + C_HEADS + (k - B_HEADS) // (C_HEADS // C_KV)
                            for t in range(TT):
                                ins = pe.matmul(ps[:, bank, t * SEQ:(t + 1) * SEQ], qkT[:, q, t * P:(t + 1) * P],
                                                qkT[:, key, :], start=True, stop=True)
                            ins.then_inc(psum_full[bank], 1)
                        if step == "flip":
                            pe.wait_ge(prob_done, layer * N_HEADS + (k + 1))
                            wait_free(pe, layer, 4, (step, k))
                            for n, (t, key) in enumerate(((0, 0), (1, 0), (1, 1))):
                                ins = pe.transpose(ps[:, 4, n * P:(n + 1) * P],
                                                   prob[:, k % 2, t, key * P:(key + 1) * P], ident[:, :])
                            ins.then_inc(psum_full[4], 1)
                        if step == "value":
                            if k == 0:
                                wait_read(pe, layer, in_banks(V_AT)[1], ("proj", V_AT))
                            wait_read(pe, layer, 4, ("flip", k))
                            wait_free(pe, layer, 5, (step, k))
                            v, h = (vB, k) if k < B_HEADS else (vC, (k - B_HEADS) // (C_HEADS // C_KV))
                            cols = slice(h * HEAD, (h + 1) * HEAD)
                            pT = probT[:, k % 2, :]
                            pe.matmul(ps[:, 5, 0:P], v[:, 0, cols], pT[:, 0:P], start=True, stop=True)
                            pe.matmul(ps[:, 5, P:SEQ], v[:, 0, cols], pT[:, P:2 * P], start=True, stop=False)
                            pe.matmul(ps[:, 5, P:SEQ], v[:, 1, cols], pT[:, 2 * P:3 * P], start=False, stop=True)\
                                .then_inc(psum_full[5], 1)
                        if step == "hout":
                            wait_read(pe, layer, in_banks(I_AT)[1], ("proj", I_AT))
                            wait_read(pe, layer, 7, ("level", LEVELS - 1))
                            wait_read(pe, layer, 6, ("level", LEVELS))
                            for t in range(TT):
                                wait_free(pe, layer, 6 + t, (step, k))
                                for h in range(A_HEADS):
                                    o, cols = ps[:, 6 + t, h * HEAD:(h + 1) * HEAD], slice(h * HEAD, (h + 1) * HEAD)
                                    if t == 1:
                                        pe.matmul(o, att01[:, h, :], iA[:, 0, cols], start=True, stop=False)
                                    ins = pe.matmul(o, att[:, h * TT + t, :], iA[:, t, cols], start=t == 0,
                                                    stop=True)
                                ins.then_inc(psum_full[6 + t], 1)
                        if step == "hturn":
                            pe.wait_ge(o_gated, layer + 1)
                            for pair in range(2):
                                wait_free(pe, layer, 4 + pair, (step, k))
                                for b in range(2):
                                    for t in range(TT):
                                        c0 = (2 * pair + b) * P
                                        ins = pe.transpose(
                                            ps[:, 4 + pair, b * SEQ + t * P:b * SEQ + (t + 1) * P],
                                            osb[:, t, c0:c0 + P], ident[:, :])
                                ins.then_inc(psum_full[4 + pair], 1)
                turn_x(layer, 1)
                ffn_chunk(layer, 0, True)
                with pe.Fori(1, NC_FF) as c:
                    ffn_chunk(layer, c, False)
                for n in range(NC_OUT * GD):
                    c, j = n // GD, n % GD
                    if n == 0:
                        pe.wait_ge(conv_done, layer * PAIRS + PAIRS)
                        pe.wait_ge(h_done, layer * PAIRS + (PAIRS - 2))
                    if n in (GD - 2, GD - 1):
                        pe.wait_ge(h_done, layer * PAIRS + (PAIRS - GD + n + 1))
                    if j == 0:
                        for b in in_banks(c):
                            wait_free(pe, layer, b, ("down", c))
                    rows_times_chunk(layer, BASE_DOWN + n, hT, (GK * j, GK * j + 1), in_banks(c), j == 0,
                                     j == GD - 1)


def attention_bias():
    lag = np.arange(SEQ)[:, None] - np.arange(SEQ)[None, :]
    count = sum(((lag >= 0) & (lag % d == 0) & (lag // d <= w // d)).astype(np.float64) for w, d in PATTERNS)
    window = (lag >= 0) & (lag < C_WINDOW)
    log_count = np.where(count > 0, np.log(np.maximum(count, 1)), NEG)
    return np.stack([log_count, np.where(window, 0.0, NEG)]).astype(np.float32)


def level_masks():
    j, i = np.arange(P)[:, None], np.arange(P)[None, :]
    masks = [j == i]
    for n in range(1, LEVELS):
        h = 2 ** (n - 1)
        masks.append((j // (2 * h) == i // (2 * h)) & (j // h % 2 == 0) & (i // h % 2 == 1))
    return np.stack(masks).astype(np.float32)


def rope_tables():
    inv = np.float32(ROPE_THETA) ** (-np.arange(0, ROPE, 2, dtype=np.float32) / np.float32(ROPE))
    angle = (np.arange(SEQ, dtype=np.float32)[:, None] * inv.astype(np.float32)[None, :]).astype(np.float64)
    cos, sin = np.cos(angle), np.sin(angle)
    return np.stack([np.concatenate([cos, cos], 1), np.concatenate([-sin, sin], 1)]).astype(np.float32)


_INS = ["x", "w_in", "lb_logits", "a_norm_w", "c_sinks", "w_out", "ln1_g", "ln1_b", "w_gate", "w_up", "conv_w",
        "conv_b", "w_down", "ln2_g", "ln2_b"]


def kernel(**inputs):
    import numpy as _np
    import concourse.bacc as _bacc
    from concourse import mybir as _mybir
    from concourse.bass_utils import run_bass_kernel_spmd as _run

    nc = _bacc.Bacc("TRN2", target_bir_lowering=False, num_devices=1)
    arrays, args = {}, []
    values = [(name, _np.ascontiguousarray(inputs[name])) for name in _INS]
    values += [("c_ident", _np.eye(P, dtype=_np.float32)), ("c_bias", attention_bias()),
               ("c_level", level_masks()), ("c_rope", rope_tables()),
               ("c_unit", _np.stack([_np.ones(D_MODEL, _np.float32), _np.zeros(D_MODEL, _np.float32)]))]
    for name, a in values:
        arrays[f"in_{name}_dram"] = a
        args.append(nc.dram_tensor(f"in_{name}_dram", a.shape, _mybir.dt.from_np(a.dtype), kind="ExternalInput").ap())
    args.append(nc.dram_tensor("out_0_dram", (1, SEQ, D_MODEL), _mybir.dt.float32, kind="ExternalOutput").ap())
    program(nc, *args)
    r = _run(nc, [arrays], core_ids=[0])
    return r.results[0]["out_0_dram"]
```

```python
import math
from contextlib import ExitStack

import concourse.bass as bass
import numpy as np
from concourse import mybir

D_MODEL, SEQ, DEPTH, HEAD, D_FF, TAPS = 2048, 256, 2, 128, 5632, 3
A_HEADS, B_HEADS, C_HEADS, C_KV = 4, 6, 6, 2
PATTERNS, C_WINDOW = ((128, 1), (512, 4), (2048, 16)), 128
IN_WIDTH = (4 * A_HEADS + 3 * B_HEADS + C_HEADS + 2 * C_KV) * HEAD
ROPE_THETA, ROPE = 500000.0, HEAD // 4
EPS = 1e-5
ALPHA = (2 * DEPTH) ** 0.25
SCALE = HEAD ** -0.5
NEG = -1e30

P = 128
TT = SEQ // P
KT = D_MODEL // P
FT = D_FF // P
CW = 512
GK = 2
GC = KT // GK
GD = FT // GK
RING = 4
NC_IN, NC_OUT, NC_FF = IN_WIDTH // CW, D_MODEL // CW, D_FF // CW
BASE_OUT = NC_IN * GC
BASE_FFN = BASE_OUT + NC_OUT * GC
BASE_DOWN = BASE_FFN + 2 * NC_FF * GC
GROUPS = BASE_DOWN + NC_OUT * GD
LAYER_FILLS = GROUPS // RING
LAG = 3
SKEW = 3
NORM_STEPS = 4
PRE = RING - SKEW

F_CHUNK, Q_CHUNK, I_CHUNK, G_CHUNK = 1, 0, 2, 3
ORDER = [F_CHUNK, Q_CHUNK] + list(range(4, NC_IN - 2)) + [NC_IN - 1, NC_IN - 2, I_CHUNK, G_CHUNK]
QB0 = 4 * A_HEADS
VB0 = QB0 + 2 * B_HEADS
QC0 = VB0 + B_HEADS
VC0 = QC0 + C_HEADS + C_KV


def qk_slot(block):
    if QB0 <= block < VB0:
        return block - QB0
    if QC0 <= block < VC0:
        return 2 * B_HEADS + block - QC0
    return None


def chunk_blocks(chunk):
    return range(4 * chunk, 4 * chunk + 4)


def parts(chunk):
    runs = []
    for name, b0, b1 in (("staged", 0, VB0), ("vB", VB0, QC0), ("staged", QC0, VC0), ("vC", VC0, 4 * NC_IN)):
        lo, hi = max(b0, 4 * chunk), min(b1, 4 * chunk + 4)
        if lo < hi:
            runs.append((name, lo, hi))
    return runs


def rope_blocks(chunk):
    return [b - 4 * chunk for b in chunk_blocks(chunk) if qk_slot(b) is not None]


def turned_pairs(chunk):
    if chunk in (F_CHUNK, Q_CHUNK):
        return [0, 1]
    return sorted({b // 2 for b in rope_blocks(chunk)})


LEVELS = 8
LEVEL_COLS = P + (LEVELS - 1) * P // 2
N_HEADS = B_HEADS + C_HEADS
MIX_ORDER = [2, 3, 4, 5, 6, 7, 0, 1]

WHEN = {("params", 0): GC + 1}
for i, chunk in enumerate(ORDER):
    WHEN["evac", i] = GC * i + 7
    if turned_pairs(chunk):
        WHEN["turn", i] = GC * (i + 1) + 3
for n in range(LEVELS + 1):
    WHEN["level", n] = 21 + 3 * n
for k, at in enumerate([46, 49, 52, 56, 59, 62, 68, 71, 76, 78, 80, 82]):
    WHEN["score", k], WHEN["finish", k], WHEN["flip", k], WHEN["value", k] = at, at + 1, at + 3, at + 5
WHEN["hout", 0], WHEN["hsquare", 0], WHEN["hscale", 0] = 84, 85, 86
WHEN["hgate", 0], WHEN["hturn", 0] = 88, 90
for n in range(GC):
    WHEN["mixsplit", n] = BASE_OUT - 4 + n + (n >= GC - 2)
for c in range(NC_OUT - 1):
    WHEN["yevac", c] = BASE_OUT + GC * c + 7
KINDS = ["params", "evac", "turn", "level", "hout", "hsquare", "hscale", "flip", "value", "finish", "score",
         "hgate", "hturn", "mixsplit", "yevac"]
STEPS = {}
for (kind, k), at in sorted(WHEN.items(), key=lambda w: (w[1], KINDS.index(w[0][0]), w[0][1])):
    STEPS.setdefault(at, []).append((kind, k))
POOL_STEPS = {}
for (kind, k), at in sorted(WHEN.items(), key=lambda w: w[1] - 3.1 * (w[0][0] == "level")):
    if kind in ("level", "evac"):
        POOL_STEPS.setdefault(at - 3 * (kind == "level"), []).append((kind, k))
TURNS = [i for i in range(len(ORDER)) if ("turn", i) in WHEN]
ROPES = [i for i in TURNS if rope_blocks(ORDER[i])]
B_TURN = max(i for i in TURNS if chunk_blocks(ORDER[i])[0] < VB0 and rope_blocks(ORDER[i]))
C_TURN = ORDER.index(NC_IN - 1)
C_TURN_LAST = ORDER.index(NC_IN - 2)
C_EARLY = 4 * (NC_IN - 2) - QC0
I_AT, G_AT = ORDER.index(I_CHUNK), ORDER.index(G_CHUNK)
V_FIRST = {max(chunk_blocks(chunk)[0], VB0) - VB0: i for i, chunk in enumerate(ORDER)
           if any(VB0 <= b < QC0 for b in chunk_blocks(chunk))}


def in_banks(i):
    return (0, 1) if i % 2 == 0 else (2, 3)


def out_banks(c):
    return in_banks(c + 1)


def bank_uses():
    uses = [[("xturn", 0)] for _ in range(8)]
    for p in range(BASE_FFN):
        if p % GC == 0:
            i = p // GC
            for b in in_banks(i) if p < BASE_OUT else out_banks(i - NC_IN):
                uses[b].append(("proj", i) if p < BASE_OUT else ("out", i - NC_IN))
        for kind, k in STEPS.get(p, ()):
            banks = {"params": (6,), "turn": None, "level": (6, 7) if k == 0 else (6 + k % 2,), "score": (6 + k % 2,),
                     "flip": (4,), "value": (5,), "hout": (6, 7), "hturn": (4, 5)}.get(kind, ())
            if kind == "turn":
                banks = [4 + pair for pair in turned_pairs(ORDER[k])]
            for b in banks:
                uses[b].append((kind, k))
    for b in range(8):
        uses[b].append(("xturn", 1))
    for c in range(NC_OUT):
        for b in in_banks(c):
            uses[b].append(("down", c))
    return uses


USES = bank_uses()
FULL = [[u for u in bank if u[0] not in ("proj", "out", "down")] for bank in USES]

PAR_LN = (2 * KT, 0)
PAR_CONV = 4 * KT
PAR_COLS = 4 * KT + (TAPS + 1) * FT
PAR_SETS = (4 * KT + FT, 2 * FT, FT)
ACT_LINKS, DVE_LINKS, POOL_LINKS, FFN_LINKS = 8, 61, 43, 8 * NC_FF
FIN_DVE = (((0, 480), (480, 960)), ((0, 640), (640, 1280)))
FIN_POOL = ((960, D_MODEL), (1280, D_MODEL))
PAIRS = 2 * NC_FF


def program(nc, x, w_in, lb_logits, a_norm_w, c_sinks, w_out, ln1_g, ln1_b, w_gate, w_up, conv_w, conv_b,
            w_down, ln2_g, ln2_b, c_ident, c_bias, c_level, c_rope, out):
    F32, F32R, U8 = mybir.dt.float32, mybir.dt.float32r, mybir.dt.uint8
    ACT, ALU, AX = mybir.ActivationFunctionType, mybir.AluOpType, mybir.AxisListType
    ctx = ExitStack()
    with ctx:
        def sb(name, shape, dt=F32):
            return ctx.enter_context(nc.sbuf_tensor(name, shape, dt))

        def sem(name):
            return ctx.enter_context(nc.semaphore(name))

        raw = sb("raw", [P, RING, GK, CW])
        whi = sb("whi", [P, RING, GK, CW], F32R)
        wlo = sb("wlo", [P, RING, GK, CW], F32R)
        xT = sb("xT", [P, KT, 2, SEQ], F32R)
        xres = sb("xres", [P, TT, D_MODEL])
        mix = sb("mix", [P, KT, SEQ])
        flat = mix[:, :, :].rearrange("p k s -> p (k s)")
        lnb = flat.rearrange("p (a d) -> p a d", a=2)
        fsum = flat[:, 0:1024].rearrange("p (q m s) -> p q m s", q=2, m=2)
        fconv = flat[:, 1024:2048].rearrange("p (q m s) -> p q m s", q=2, m=2)
        fsilu = flat[:, 2048:3072].rearrange("p (q m s) -> p q m s", q=2, m=2)
        ident = sb("ident", [P, P])
        parT = sb("parT", [P, PAR_COLS])
        conv = parT[:, PAR_CONV:].rearrange("p (a f) -> p a f", f=FT)
        parC = sb("parC", [P, TAPS + 1, 4])
        rope = sb("rope", [P, 2, TT, ROPE])
        sinks = sb("sinks", [P, N_HEADS])
        lbw = sb("lbw", [P, 6, DEPTH, A_HEADS])
        lbc = sb("lbc", [P, 2, 1, A_HEADS])
        stats = sb("stats", [P, TT, NC_OUT, 6])
        mv = sb("mv", [P, TT, 2])
        lns = sb("lns", [P, 3, TT])
        hd = sb("hd", [P, 2, 5, TT])
        hs = sb("hs", [P, 4, TT * A_HEADS])
        anorm = sb("anorm", [P, HEAD])
        spare = sb("spare", [P, 10 + LEVELS])
        arena_base = (nc.sbuf_base + 31) // 32 * 32
        ctx.enter_context(nc.sbuf_tensor("arena", [P, FT * 2 * SEQ], F32))
        hT = nc.alloc_sbuf_tensor_at("hT", [P, FT, 2, SEQ], F32R, offset=arena_base)
        place = [arena_base]

        def at(name, shape, dt=F32, size=4):
            t = nc.alloc_sbuf_tensor_at(name, shape, dt, offset=place[0])
            place[0] += int(np.prod(shape[1:])) * size
            assert place[0] <= arena_base + FT * 2 * SEQ * 4, place[0] - arena_base
            return t

        qT = at("qT", [P, A_HEADS, SEQ])
        kT = at("kT", [P, A_HEADS, SEQ])
        pre = at("pre", [P, A_HEADS, SEQ])
        suf = at("suf", [P, A_HEADS, SEQ])
        ql = at("ql", [P, A_HEADS, SEQ])
        kl = at("kl", [P, A_HEADS, SEQ])
        att = at("att", [P, A_HEADS * TT, P])
        att01 = at("att01", [P, A_HEADS, P])
        iA = at("iA", [P, TT, CW])
        gA = at("gA", [P, TT, CW])
        qkT = at("qkT", [P, 2 * B_HEADS + C_HEADS + C_KV, SEQ])
        vB = at("vB", [P, TT, B_HEADS * HEAD])
        vC = at("vC", [P, TT, C_KV * HEAD])
        staged = at("staged", [P, 2, TT, CW])
        prob = at("prob", [P, 2, 3 * P])
        probT = at("probT", [P, 2, 3 * P])
        bias = at("bias", [P, 2, 3 * P])
        level = at("level", [P, LEVEL_COLS], U8, 1)
        ropetmp = at("ropetmp", [P, TT, 4 * ROPE])
        aff = qkT[:, 0:4, :].rearrange("p (i k) s -> p i k s", i=2)
        att_flat = att[:, :, :].rearrange("p a s -> p (a s)")
        osb = pre[:, :, :].rearrange("p h s -> p (h s)").rearrange("p (t c) -> p t c", t=TT)
        osq = suf[:, :, :].rearrange("p h s -> p (h s)").rearrange("p (t c) -> p t c", t=TT)
        heads = lambda m: m.rearrange("p t (h c) -> p (t h) c", c=HEAD)
        par_rows = prob[:, 0, :].rearrange("p (a c) -> p a c", a=3)
        keys = (slice(0, P), slice(P, 3 * P))
        lb_rows = staged[:, 0, 0, 0:P]

        ps = ctx.enter_context(nc.psum_tensor("ps", [P, 8, CW], F32))

        raw_in = [sem(f"raw_in{s}") for s in range(RING)]
        hi_done, lo_done, pe_used = sem("hi_done"), sem("lo_done"), sem("pe_used")
        psum_full = [sem(f"psum_full{b}") for b in range(8)]
        psum_free = [sem(f"psum_free{b}") for b in range(8)]
        x_in = [sem(f"x_in{c}") for c in range(NC_OUT)]
        const_in, rope_in, lb_in = sem("const_in"), sem("rope_in"), sem("lb_in")
        masks_in, params_in, small_in = sem("masks_in"), sem("params_in"), sem("small_in")
        ln1_in, ln2_in = sem("ln1_in"), sem("ln2_in")
        unit_par = sem("unit_par")
        lb_turned, lb_max, lb_exp = sem("lb_turned"), sem("lb_max"), sem("lb_exp")
        xhi_done, x_ready, natural = sem("xhi_done"), sem("x_ready"), sem("natural")
        rope_done, f_ready, qk_ready = sem("rope_done"), sem("f_ready"), sem("qk_ready")
        max_done, exp_done, prob_done = sem("max_done"), sem("exp_done"), sem("prob_done")
        ovar_done, ostd_done, gate_done, o_gated = (sem("ovar_done"), sem("ostd_done"), sem("gate_done"),
                                                    sem("o_gated"))
        ln_var, ln_std, ln_done = sem("ln_var"), sem("ln_std"), sem("ln_done")
        half_done, conv_done, silu_done = sem("half_done"), sem("conv_done"), sem("silu_done")
        h_full, h_hi, h_done = sem("h_full"), sem("h_hi"), sem("h_done")
        act_link, dve_link, pool_link, ffn_link = (sem("act_link"), sem("dve_link"), sem("pool_link"),
                                                   sem("ffn_link"))
        taps_done, fin_pool = sem("taps_done"), sem("fin_pool")
        first_tile, ln_scale, ln_act = sem("first_tile"), sem("ln_scale"), sem("ln_act")
        fin_done, out_done, first_rows = sem("fin_done"), sem("out_done"), sem("first_rows")

        CREDIT = RING

        def wait_full(eng, layer, bank, use):
            eng.wait_ge(psum_full[bank], layer * len(FULL[bank]) + (FULL[bank].index(use) + 1))

        def wait_free(pe, layer, bank, use):
            pe.wait_ge(psum_free[bank], layer * len(USES[bank]) + (USES[bank].index(use) + 1))

        def wait_read(eng, layer, bank, use):
            eng.wait_ge(psum_free[bank], layer * len(USES[bank]) + (USES[bank].index(use) + 2))

        def wait_groups(eng, layer, n):
            eng.wait_ge(pe_used, layer * GROUPS + (n + CREDIT))

        def carry_wait(eng, n):
            if eng is nc.vector:
                eng.memset(spare[:, n:n + 1], 0.0)
            else:
                eng.tensor_tensor(spare[:, n:n + 1], spare[:, 0:1], spare[:, 0:1], ALU.add)

        class Link:

            def __init__(self, eng, semaphore):
                self.eng, self.sem, self.base, self.n = eng, semaphore, 0, 0

            def __call__(self, ins):
                self.n += 1
                ins.then_inc(self.sem, 1)
                self.eng.wait_ge(self.sem, self.base + self.n)

        def x_quarter(c):
            return x[:, :, c * CW:(c + 1) * CW].rearrange("b (t p) d -> p (b t) d", p=P)

        block = ctx.enter_context(nc.Block())

        @block.sync
        def _(sp):
            sp.dma_start(ident[:, :], c_ident[:, :]).then_inc(const_in, 16)
            sp.dma_start(lb_rows[0:DEPTH * A_HEADS, :], lb_logits.rearrange("l (h k) -> (l h) k", k=P))\
                .then_inc(lb_in, 16)

            def load(w, layer, moving, n, row, col):
                s = n % RING
                sp.wait_ge(lo_done, layer * GROUPS + moving + (n + 1 - RING + CREDIT))
                if row == 0:
                    sp.sem_inc(first_rows, 1)
                src = w[bass.ds(layer, 1), row * P:(row + GK) * P, bass.ds(col, CW)]
                sp.dma_start(raw[:, s, :, :], src.rearrange("l (k p) n -> p (l k) n", p=P)).then_inc(raw_in[s], 16)

            with sp.Fori(0, DEPTH) as layer:
                for i, chunk in enumerate(ORDER[:2]):
                    for j in range(GC):
                        load(w_in, layer, 0, i * GC + j, j * GK, chunk * CW)
                with sp.Fori(4, NC_IN - 2) as chunk:
                    for j in range(GC):
                        load(w_in, layer, chunk * GC, j - 2 * GC, j * GK, chunk * CW)
                for i in range(NC_IN - 4, NC_IN):
                    for j in range(GC):
                        load(w_in, layer, 0, i * GC + j, j * GK, ORDER[i] * CW)
                with sp.Fori(0, NC_OUT) as c:
                    for j in range(GC):
                        load(w_out, layer, c * GC, BASE_OUT + j, MIX_ORDER[j] * GK, c * CW)
                with sp.Fori(0, NC_FF) as c:
                    for half, w in enumerate((w_gate, w_up)):
                        for j in range(GC):
                            load(w, layer, c * (2 * GC), BASE_FFN + half * GC + j, j * GK, c * CW)
                with sp.Fori(0, NC_OUT // 2) as two:
                    for half in range(2):
                        col = sp.snap(two * (2 * CW) + half * CW)
                        for j in range(GD):
                            load(w_down, layer, two * (2 * GD), BASE_DOWN + half * GD + j, j * GK, col)
            rows = out.rearrange("b (t p) d -> (b t) p d", p=P)
            for t in range(TT):
                for n in ((-1, 0, 1), (0, -1, 1))[t]:
                    c0, c1 = FIN_POOL[t] if n < 0 else FIN_DVE[t][n]
                    if n < 0:
                        sp.wait_ge(fin_pool, t + 1)
                    else:
                        sp.wait_ge(fin_done, len(FIN_DVE[t]) * t + n + 1)
                    sp.dma_start(rows[t, :, c0:c1], xres[:, t, c0:c1]).then_inc(out_done, 16)
            sp.wait_ge(out_done, 16 * TT * (len(FIN_DVE[0]) + 1))

        @block.gpsimd
        def _(pool):
            link = Link(pool, pool_link)
            pool.memset(spare[:, 0:1], 0.0)
            pool.memset(sinks[:, 0:B_HEADS], NEG)
            pool.memset(parT[:, PAR_LN[0]:PAR_LN[0] + KT], 1.0)
            pool.memset(parT[:, PAR_LN[0] + KT:PAR_LN[0] + 2 * KT], 0.0).then_inc(unit_par, 1)
            pool.memset(lnb[:, 0, :], 1.0)
            pool.memset(lnb[:, 1, :], 0.0).then_inc(unit_par, 1)
            pool.wait_ge(unit_par, 2)

            def row(a, layer):
                return a[bass.ds(layer, 1), :]

            def natural_affine(layer, which):
                for b in range(8):
                    wait_full(pool, layer, b, ("xturn", which))
                if which == 1:
                    pool.wait_ge(ln1_in, layer * 32 + 32)
                for t in range(TT):
                    link(pool.tensor_tensor(xres[:, t, :], xres[:, t, :], lnb[:, 0, :], ALU.mult))
                    pool.tensor_tensor(xres[:, t, :], xres[:, t, :], lnb[:, 1, :], ALU.add).then_inc(natural, 1)

            with pool.Fori(0, DEPTH) as layer:
                link.base, link.n = layer * POOL_LINKS, 0
                wait_groups(pool, layer, 0)
                carry_wait(pool, 1)
                pool.dma_start(bias[:, :, :], c_bias.rearrange("a p s -> p a s")).then_inc(masks_in, 16)
                pool.dma_start(att_flat[:, 0:LEVEL_COLS], c_level[:, :]).then_inc(masks_in, 16)
                for n, a in enumerate((ln1_g, ln1_b, ln2_g, ln2_b)):
                    pool.dma_start(par_rows[n * KT:(n + 1) * KT, 0, :],
                                   row(a, layer).rearrange("l (k p) -> (l k) p", p=P)).then_inc(params_in, 16)
                for (r, n), a in zip(((4 * KT, 0), (0, 1), (FT, 1), (0, 2)),
                                     [conv_w[bass.ds(layer, 1), j, :] for j in range(TAPS)] + [row(conv_b, layer)]):
                    pool.dma_start(par_rows[r:r + FT, n, :], a.rearrange("l (k p) -> (l k) p", p=P))\
                        .then_inc(params_in, 16)
                pool.dma_start(anorm[:, :], row(a_norm_w, layer).broadcast_to([P, HEAD])).then_inc(small_in, 16)
                pool.dma_start(sinks[:, B_HEADS:N_HEADS], row(c_sinks, layer).broadcast_to([P, C_HEADS]))\
                    .then_inc(small_in, 16)
                natural_affine(layer, 0)
                pool.memset(suf[:, :, :], 1.0)
                pool.memset(ql[:, :, :], 0.0)
                link(pool.memset(kl[:, :, :], 0.0))

                for p in range(BASE_FFN):
                    for step, k in POOL_STEPS.get(p, ()):
                        if step == "evac" and rope_blocks(ORDER[k]):
                            if k == ROPES[0]:
                                pool.wait_ge(rope_in, 16)
                            wait_read(pool, layer, in_banks(k)[1], ("proj", k))
                            b0, nb = rope_blocks(ORDER[k])[0], len(rope_blocks(ORDER[k]))
                            half = ROPE // 2
                            if k != ROPES[0]:
                                pool.wait_ge(rope_done, layer * (TT * len(ROPES)) + TT * ROPES.index(k))
                            for t in range(TT):
                                v = staged[:, k % 2, t, b0 * P:(b0 + nb) * P].rearrange("p (b c) -> p b c", c=P)
                                tmp = ropetmp[:, t, 0:nb * ROPE].rearrange("p (b c) -> p b c", c=ROPE)
                                cos, sin = (rope[:, a, t, :].unsqueeze(1).broadcast_to([P, nb, ROPE])
                                            for a in (0, 1))
                                pool.tensor_tensor(tmp[:, :, 0:half], v[:, :, half:ROPE], sin[:, :, 0:half],
                                                   ALU.mult)
                                link(pool.tensor_tensor(tmp[:, :, half:ROPE], v[:, :, 0:half],
                                                        sin[:, :, half:ROPE], ALU.mult))
                                link(pool.tensor_tensor(v[:, :, 0:ROPE], v[:, :, 0:ROPE], cos, ALU.mult))
                                pool.tensor_tensor(v[:, :, 0:ROPE], v[:, :, 0:ROPE], tmp, ALU.add)\
                                    .then_inc(rope_done, 1)
                        if step == "level" and k >= 1:
                            h = 2 ** (k - 1)
                            if k == 1:
                                pool.wait_ge(f_ready, layer + 1)
                                wait_read(pool, layer, 5, ("turn", 1))
                            else:
                                wait_full(pool, layer, 6 + (k - 1) % 2, ("level", k - 1))
                            first, second = (lambda m, a=a: m[:, :, :].rearrange(
                                "p a (n two h) -> p (a n) two h", two=2, h=h)[:, :, a, :] for a in (0, 1))
                            pool.tensor_tensor(second(ql), second(qT), second(pre), ALU.mult)
                            pool.tensor_tensor(first(kl), first(kT), first(suf), ALU.mult).then_inc(qk_ready, 1)
                            if k < LEVELS:
                                pool.wait_ge(qk_ready, layer * LEVELS + k)
                                shape = [P, A_HEADS * SEQ // (2 * h), h]
                                link(pool.tensor_tensor(first(suf), first(suf),
                                                        second(pre)[:, :, h - 1:h].broadcast_to(shape), ALU.mult))
                                link(pool.tensor_tensor(second(pre), second(pre),
                                                        first(pre)[:, :, h - 1:h].broadcast_to(shape), ALU.mult))
                        if step == "evac" and k == G_AT:
                            wait_read(pool, layer, in_banks(k)[1], ("proj", k))
                            pool.wait_ge(small_in, layer * 32 + 32)
                            gain = anorm[:, :].unsqueeze(1).broadcast_to([P, TT * A_HEADS, HEAD])
                            pool.tensor_tensor(heads(gA[:, :, :]), heads(gA[:, :, :]), gain, ALU.mult)\
                                .then_inc(gate_done, 1)
                pool.wait_ge(x_ready, layer * 24 + 16)
                carry_wait(pool, 2)
                pool.dma_start(lnb[:, 0, :], row(ln1_g, layer).broadcast_to([P, D_MODEL])).then_inc(ln1_in, 16)
                pool.dma_start(lnb[:, 1, :], row(ln1_b, layer).broadcast_to([P, D_MODEL])).then_inc(ln1_in, 16)
                natural_affine(layer, 1)
                pool.wait_ge(h_done, layer * PAIRS + PAIRS)
                carry_wait(pool, 3)
                pool.dma_start(lnb[:, 0, :], row(ln2_g, layer).broadcast_to([P, D_MODEL])).then_inc(ln2_in, 16)
                pool.dma_start(lnb[:, 1, :], row(ln2_b, layer).broadcast_to([P, D_MODEL])).then_inc(ln2_in, 16)
                pool.wait_ge(ln2_in, layer * 32 + 32)
            assert link.n == POOL_LINKS, link.n
            link.base = DEPTH * POOL_LINKS - link.n
            for t in range(TT):
                c0, c1 = FIN_POOL[t]
                pool.wait_ge(ln_done, CREDIT + NORM_STEPS * (2 * DEPTH - 1) + (1, NORM_STEPS)[t])
                if t == 0:
                    pool.wait_ge(ln_act, CREDIT + 2 * DEPTH)
                link(pool.tensor_tensor(xres[:, t, c0:c1], xres[:, t, c0:c1], lnb[:, 0, c0:c1], ALU.mult))
                pool.tensor_tensor(xres[:, t, c0:c1], xres[:, t, c0:c1], lnb[:, 1, c0:c1], ALU.add)\
                    .then_inc(fin_pool, 1)

        @block.scalar
        def _(act):
            link = Link(act, act_link)
            for c in range(2):
                act.dma_start(xres[:, :, c * CW:(c + 1) * CW], x_quarter(c)).then_inc(x_in[c], 16)
            act.wait_ge(unit_par, 1)
            act.activation(spare[:, 9 + LEVELS:10 + LEVELS], spare[:, 0:1], ACT.Exp)
            for c in range(2, NC_OUT):
                act.dma_start(xres[:, :, c * CW:(c + 1) * CW], x_quarter(c)).then_inc(x_in[c], 16)
            act.dma_start(rope[:, :, :, :], c_rope.rearrange("a (t p) r -> p a t r", p=P)).then_inc(rope_in, 16)
            act.wait_ge(lb_max, 1)
            act.activation(lbw[:, 1, :, :], lbw[:, 0, :, :], ACT.Exp).then_inc(lb_exp, 1)

            def split_hi(layer, moving, n):
                s = n % RING
                act.wait_ge(raw_in[s], layer * (LAYER_FILLS * 16) + fills(moving) + (n // RING + 1) * 16)
                wait_groups(act, layer, moving + (n + 1 - RING))
                act.activation(whi[:, s, :, :], raw[:, s, :, :], ACT.Copy).then_inc(hi_done, 1)

            def fills(moving):
                return moving * (16 // RING)

            def x_affine(layer, which, b):
                number = layer * 24 + 16 * which + b
                if which == 0 and b == 0:
                    act.wait_ge(unit_par, 1)
                if b >= 2:
                    act.wait_ge(x_ready, number - 1)
                wait_full(act, layer, b, ("xturn", which))
                for kk in range(2):
                    col = PAR_LN[which] + 2 * b + kk
                    ins = act.activation(aff[:, b % 2, kk, :], ps[:, b, kk * SEQ:(kk + 1) * SEQ], ACT.Identity,
                                         scale=parT[:, col:col + 1], bias=parT[:, col + KT:col + KT + 1])
                ins.then_inc(psum_free[b], 1)

            def norm(layer, which):
                act.activation(spare[:, 9 + LEVELS:10 + LEVELS], spare[:, 0:1], ACT.Sqrt)
                for t in range(TT):
                    act.wait_ge(ln_var, layer * 4 + (2 * which + t + 1))
                    act.activation(lns[:, 1, t:t + 1], lns[:, 0, t:t + 1], ACT.Sqrt).then_inc(ln_std, 1)
                    if t == 0:
                        act.wait_ge(ln_scale, layer * 2 + (which + 1))
                        act.activation(xres[:, t, D_MODEL // 2:], xres[:, t, D_MODEL // 2:], ACT.Identity,
                                       scale=lns[:, 2, t:t + 1], bias=lns[:, 0, t:t + 1]).then_inc(ln_act, 1)
                        if which == 0:
                            for n in range(PRE, LAG):
                                split_hi(layer, 0, BASE_FFN + n)

            def low_sum(layer, c, half, q):
                wait_groups(act, layer, c * (2 * GC) + (BASE_FFN + (half + 1) * GC))
                if half == 0:
                    act.wait_ge(natural, layer * 4 + 4)
                b = 4 * half + 2 * q
                act.activation(fsum[:, q, :, :], ps[:, b:b + 2, SEQ:2 * SEQ], ACT.Copy).then_inc(half_done, 1)

            def silu(layer, c, q):
                act.wait_ge(conv_done, layer * PAIRS + c * 2 + (q + 1))
                act.activation(fsilu[:, q, :, :], fconv[:, q, :, :], ACT.Silu).then_inc(silu_done, 1)

            def hidden_hi(layer, c, q):
                act.wait_ge(h_full, layer * PAIRS + c * 2 + (q + 1))
                act.activation(hT[:, bass.ds(c * 4 + 2 * q, 2), 0, :], fconv[:, q, :, :], ACT.Copy)\
                    .then_inc(h_hi, 1)

            def ffn_chunk(layer, c, first):
                for j in range(GC):
                    if first:
                        x_affine(layer, 1, j)
                    if not first or j >= LAG:
                        split_hi(layer, c * (2 * GC), BASE_FFN + j)
                    if not first:
                        if j in (3, 5):
                            low_sum(layer, c - 1, 1, (j - 3) // 2)
                        if j in (4, 6):
                            hidden_hi(layer, c - 1, (j - 4) // 2)
                for j in range(GC):
                    split_hi(layer, c * (2 * GC), BASE_FFN + GC + j)
                    if j in (3, 5):
                        low_sum(layer, c, 0, (j - 3) // 2)
                    if j in (4, 6):
                        silu(layer, c, (j - 4) // 2)

            with act.Fori(0, DEPTH) as layer:
                link.base, link.n = layer * ACT_LINKS, 0
                for p in range(BASE_FFN + PRE):
                    if p < 8:
                        x_affine(layer, 0, p)
                    split_hi(layer, 0, p)
                    for step, k in STEPS.get(p - LAG, ()):
                        if step == "evac":
                            chunk = ORDER[k]
                            wait_groups(act, layer, GC * (k + 1))
                            for t in range(TT):
                                src = ps[:, in_banks(k)[t], :]
                                if chunk == I_CHUNK:
                                    last = act.activation(iA[:, t, :], src, ACT.Copy)
                                elif chunk == G_CHUNK:
                                    last = act.activation(gA[:, t, :], src, ACT.Silu)
                                else:
                                    for dst, b0, b1 in parts(chunk):
                                        c0 = 4 * chunk
                                        src_cols = slice((b0 - c0) * P, (b1 - c0) * P)
                                        if dst == "vB":
                                            to = vB[:, t, (b0 - VB0) * P:(b1 - VB0) * P]
                                        elif dst == "vC":
                                            to = vC[:, t, (b0 - VC0) * P:(b1 - VC0) * P]
                                        else:
                                            to = staged[:, k % 2, t, src_cols]
                                        last = act.activation(to, src[:, src_cols], ACT.Copy)
                                last.then_inc(psum_free[in_banks(k)[t]], 1)
                        if step == "turn":
                            for pair in turned_pairs(ORDER[k]):
                                wait_full(act, layer, 4 + pair, (step, k))
                                src = ps[:, 4 + pair, :].rearrange("p (b s) -> p b s", b=2)
                                if ORDER[k] == F_CHUNK:
                                    ins = act.activation(pre[:, 2 * pair:2 * pair + 2, :], src, ACT.Sigmoid)
                                elif ORDER[k] == Q_CHUNK:
                                    ins = act.activation(qT[:, 2 * pair:2 * pair + 2, :], src, ACT.Silu)
                                else:
                                    slot = qk_slot(4 * ORDER[k] + 2 * pair)
                                    ins = act.activation(qkT[:, slot:slot + 2, :], src, ACT.Copy)
                                ins.then_inc(psum_free[4 + pair], 1)
                        if step == "score":
                            act.wait_ge(max_done, layer * N_HEADS + (k + 1))
                            i = k % 2
                            for t in range(TT):
                                act.activation(prob[:, i, keys[t]], prob[:, i, keys[t]], ACT.Exp,
                                               bias=hd[:, i, 1, t:t + 1], accum_out=hd[:, i, 2, t:t + 1])
                            act.activation(hd[:, i, 3, :], hd[:, i, 1, :], ACT.Exp, bias=sinks[:, k:k + 1])\
                                .then_inc(exp_done, 1)
                        if step == "value":
                            wait_full(act, layer, 5, (step, k))
                            if k == 0:
                                act.wait_ge(natural, layer * 4 + 2)
                            act.activation(mix[:, A_HEADS + k, :], ps[:, 5, 0:SEQ], ACT.Copy)\
                                .then_inc(psum_free[5], 1)
                        if step == "hout":
                            for t in range(TT):
                                wait_full(act, layer, 6 + t, (step, k))
                                act.activation(osb[:, t, :], ps[:, 6 + t, :], ACT.Copy).then_inc(psum_free[6 + t], 1)
                        if step == "hsquare":
                            act.wait_ge(ovar_done, layer + 1)
                            act.activation(hs[:, 2, :], hs[:, 1, :], ACT.Sqrt).then_inc(ostd_done, 1)
                        if step == "hturn":
                            for pair in range(2):
                                wait_full(act, layer, 4 + pair, (step, k))
                                act.activation(mix[:, 2 * pair:2 * pair + 2, :],
                                               ps[:, 4 + pair, :].rearrange("p (b s) -> p b s", b=2), ACT.Copy)\
                                    .then_inc(psum_free[4 + pair], 1)
                        if step == "mixsplit":
                            b = MIX_ORDER[k]
                            wait_groups(act, layer, BASE_OUT - GC + b + 1)
                            if b < 2:
                                wait_read(act, layer, 4 + b, ("hturn", 0))
                            else:
                                wait_read(act, layer, 5, ("value", 2 * b + 1 - A_HEADS))
                            act.activation(xT[:, 2 * b:2 * b + 2, 0, :], mix[:, 2 * b:2 * b + 2, :], ACT.Copy)\
                                .then_inc(xhi_done, 1)
                norm(layer, 0)
                ffn_chunk(layer, 0, True)
                with act.Fori(1, NC_FF) as c:
                    ffn_chunk(layer, c, False)
                for n in range(NC_OUT * GD):
                    split_hi(layer, 0, BASE_DOWN + n)
                    if n in (3, 5):
                        low_sum(layer, NC_FF - 1, 1, (n - 3) // 2)
                    if n in (4, 6):
                        hidden_hi(layer, NC_FF - 1, (n - 4) // 2)
                norm(layer, 1)

        @block.vector
        def _(dve):
            link = Link(dve, dve_link)
            for b in range(7):
                dve.nop().then_inc(psum_free[b], 1)
            dve.nop().then_inc(lo_done, CREDIT)
            dve.nop().then_inc(ln_done, CREDIT)
            dve.nop().then_inc(ln_act, CREDIT)
            dve.wait_ge(lb_turned, 1)
            logits, e, t0, cum, low, rest = (lbw[:, a, :, :] for a in range(6))
            dve.tensor_copy(logits, ps[:, 7, 0:DEPTH * A_HEADS].rearrange("p (l h) -> p l h", l=DEPTH))\
                .then_inc(psum_free[7], 1)
            dve.wait_ge(psum_free[7], 1)
            link(dve.reduce_max(t0[:, 0, :], logits.rearrange("p l h -> p h l"), AX.X))
            dve.tensor_tensor(logits, logits, t0[:, 0:1, :].broadcast_to([P, DEPTH, A_HEADS]), ALU.subtract)\
                .then_inc(lb_max, 1)
            dve.wait_ge(lb_exp, 1)
            link(dve.reduce_sum(t0[:, 0, :], e.rearrange("p l h -> p h l"), AX.X))
            link(dve.reciprocal(t0[:, 1, :], t0[:, 0, :]))
            link(dve.tensor_tensor(e, e, t0[:, 1:2, :].broadcast_to([P, DEPTH, A_HEADS]), ALU.mult))
            link(dve.tensor_copy(cum[:, 0, :], e[:, 0, :]))
            for n in range(1, DEPTH):
                link(dve.tensor_tensor(cum[:, n, :], cum[:, n - 1, :], e[:, n, :], ALU.add))
            link(dve.tensor_tensor(low, cum, cum[:, 0:1, :].broadcast_to([P, DEPTH, A_HEADS]), ALU.subtract))
            link(dve.tensor_scalar(rest, low, -1.0, 1.0, ALU.mult, ALU.add))
            before = link.n

            def split_lo(layer, moving, n):
                s = n % RING
                dve.wait_ge(hi_done, layer * GROUPS + moving + (n + 1))
                dve.tensor_tensor(wlo[:, s, :, :], raw[:, s, :, :], whi[:, s, :, :].bitcast(F32), ALU.subtract)\
                    .then_inc(lo_done, 1)

            def x_split(layer, which, b):
                wait_read(dve, layer, b, ("xturn", which))
                dve.tensor_copy(xT[:, 2 * b:2 * b + 2, 0, :], aff[:, b % 2, :, :]).then_inc(xhi_done, 1)
                low_part(layer, 16 * which + b, 2 * b, aff[:, b % 2, :, :])

            def low_part(layer, n, kt, whole):
                dve.wait_ge(xhi_done, layer * 24 + (n + 1))
                dve.tensor_tensor(xT[:, kt:kt + 2, 1, :], whole, xT[:, kt:kt + 2, 0, :].bitcast(F32),
                                  ALU.subtract).then_inc(x_ready, 1)

            def y_chunk(layer, which, c, banks):
                use = ("out", "down")[which]
                wait_groups(dve, layer, BASE_OUT + GC * (c + 1) if which == 0 else BASE_DOWN + GD * (c + 1))
                if c == 0:
                    dve.wait_ge(natural, layer * 4 + 2 * (which + 1))
                cols = slice(c * CW, (c + 1) * CW)
                for t in range(TT):
                    dve.scalar_tensor_tensor(xres[:, t, cols], xres[:, t, cols], ALPHA, ps[:, banks[t], :],
                                             ALU.mult, ALU.add).then_inc(psum_free[banks[t]], 1)
                for t in range(TT):
                    wait_read(dve, layer, banks[t], (use, c))
                    last = dve.bn_stats(stats[:, t, c, :], xres[:, t, cols])
                link(last)

            def last_chunk_and_norm(layer, which):
                c, banks = NC_OUT - 1, (out_banks, in_banks)[which](NC_OUT - 1)
                cols = slice(c * CW, (c + 1) * CW)
                for t in range(TT):
                    if t == 0:
                        dve.wait_ge(first_tile, layer * 2 + (which + 1))
                    else:
                        wait_groups(dve, layer, (BASE_FFN, GROUPS)[which])
                    dve.scalar_tensor_tensor(xres[:, t, cols], xres[:, t, cols], ALPHA, ps[:, banks[t], :],
                                             ALU.mult, ALU.add).then_inc(psum_free[banks[t]], 1)
                    wait_read(dve, layer, banks[t], (("out", "down")[which], c))
                    link(dve.bn_stats(stats[:, t, c, :], xres[:, t, cols]))
                    carry_wait(dve, 4 + which)
                    link(dve.bn_aggr(mv[:, t, :], stats[:, t, :, :].rearrange("p c s -> p (c s)")))
                    dve.tensor_scalar(lns[:, 0, t:t + 1], mv[:, t, 1:2], EPS, None, ALU.add).then_inc(ln_var, 1)
                    dve.wait_ge(ln_std, layer * 4 + (2 * which + t + 1))
                    link(dve.reciprocal(lns[:, 2, t:t + 1], lns[:, 1, t:t + 1]))
                    if t == 0:
                        dve.scalar_tensor_tensor(lns[:, 0, t:t + 1], mv[:, t, 0:1], -1.0, lns[:, 2, t:t + 1],
                                                 ALU.mult, ALU.mult).then_inc(ln_scale, 1)
                    for c0, c1 in (((0, 2 * CW),), ((0, CW), (CW, 2 * CW), (2 * CW, D_MODEL)))[t]:
                        dve.tensor_scalar(xres[:, t, c0:c1], xres[:, t, c0:c1], mv[:, t, 0:1],
                                          lns[:, 2, t:t + 1], ALU.subtract, ALU.mult).then_inc(ln_done, 1)

            def own(layer, c, n):
                dve.wait_ge(ffn_link, layer * FFN_LINKS + c * 8 + n)

            def gate(layer, c, q):
                dve.wait_ge(half_done, layer * (2 * PAIRS) + c * 4 + (q + 1))
                b = 2 * q
                g, y = fsum[:, q, :, :], fconv[:, q, :, :]
                dve.tensor_tensor(g, ps[:, b:b + 2, 0:SEQ], g, ALU.add).then_inc(ffn_link, 1)
                own(layer, c, 3 * q + 1)
                tap = lambda j, m: parC[:, j, 2 * q + m:2 * q + m + 1]
                for m in range(2):
                    ins = dve.tensor_scalar(y[:, m, :], g[:, m, :], tap(TAPS - 1, m), tap(TAPS, m),
                                            ALU.mult, ALU.add)
                ins.then_inc(ffn_link, 1)
                own(layer, c, 3 * q + 2)
                for m in range(2):
                    ins = dve.scalar_tensor_tensor(y[:, m, 1:], g[:, m, 0:SEQ - 1], tap(1, m), y[:, m, 1:],
                                                   ALU.mult, ALU.add)
                ins.then_inc(ffn_link, 1)
                own(layer, c, 3 * q + 3)
                for m in range(2):
                    ins = dve.scalar_tensor_tensor(y[:, m, 2:], g[:, m, 0:SEQ - 2], tap(0, m), y[:, m, 2:],
                                                   ALU.mult, ALU.add)
                ins.then_inc(conv_done, 1)

            def up(layer, c, q):
                dve.wait_ge(half_done, layer * (2 * PAIRS) + c * 4 + (q + 3))
                b = 4 + 2 * q
                u = fsum[:, q, :, :]
                dve.tensor_tensor(u, ps[:, b:b + 2, 0:SEQ], u, ALU.add).then_inc(ffn_link, 1)
                own(layer, c, 7 + q)
                dve.wait_ge(silu_done, layer * PAIRS + c * 2 + (q + 1))
                dve.tensor_tensor(fconv[:, q, :, :], u, fsilu[:, q, :, :], ALU.mult).then_inc(h_full, 1)

            def hidden_lo(layer, c, q):
                dve.wait_ge(h_hi, layer * PAIRS + c * 2 + (q + 1))
                tiles = bass.ds(c * 4 + 2 * q, 2)
                dve.tensor_tensor(hT[:, tiles, 1, :], fconv[:, q, :, :], hT[:, tiles, 0, :].bitcast(F32),
                                  ALU.subtract).then_inc(h_done, 1)

            def ffn_chunk(layer, c, first):
                for j in range(GC):
                    if first:
                        x_split(layer, 1, j)
                    if not first or j >= PRE:
                        split_lo(layer, c * (2 * GC), BASE_FFN + j)
                    if not first:
                        if j in (3, 5):
                            up(layer, c - 1, (j - 3) // 2)
                        if j in (5, 7):
                            hidden_lo(layer, c - 1, (j - 5) // 2)
                if not first:
                    dve.wait_ge(conv_done, layer * PAIRS + c * 2)
                dve.tensor_copy(parC[:, :, :], conv[:, :, bass.ds(c * 4, 4)]).then_inc(taps_done, 1)
                for j in range(GC):
                    split_lo(layer, c * (2 * GC), BASE_FFN + GC + j)
                    if j == 3:
                        dve.wait_ge(taps_done, layer * NC_FF + c + 1)
                        if not first:
                            dve.wait_ge(h_done, layer * PAIRS + c * 2)
                    if j in (3, 5):
                        gate(layer, c, (j - 3) // 2)

            with dve.Fori(0, DEPTH) as layer:
                link.base, link.n = layer * DVE_LINKS + before, 0
                for p in range(BASE_FFN + PRE):
                    if p < 8:
                        x_split(layer, 0, p)
                    split_lo(layer, 0, p)
                    for step, k in STEPS.get(p - LAG, ()):
                        if step == "params":
                            dve.wait_ge(masks_in, layer * 32 + 32)
                            dve.tensor_copy(level[:, :], att_flat[:, 0:LEVEL_COLS])
                            wait_full(dve, layer, 6, (step, k))
                            dve.tensor_copy(parT[:, :], ps[:, 6, 0:PAR_COLS]).then_inc(psum_free[6], 1)
                        if step == "turn" and ORDER[k] == F_CHUNK:
                            link(dve.tensor_copy(lbc[:, :, :, :], lbw[:, 4:6, bass.ds(layer, 1), :]))
                            wait_read(dve, layer, 5, (step, k))
                            for h in range(A_HEADS):
                                last = dve.tensor_scalar(pre[:, h, :], pre[:, h, :], lbc[:, 1, 0, h:h + 1],
                                                         lbc[:, 0, 0, h:h + 1], ALU.mult, ALU.add)
                            link(last)
                            dve.tensor_scalar(kT[:, :, :], pre[:, :, :], -1.0, 1.0, ALU.mult, ALU.add)\
                                .then_inc(f_ready, 1)
                            link(dve.memset(att[:, :, :], 0.0))
                        if step == "level" and k == 0:
                            for b in (6, 7):
                                wait_full(dve, layer, b, (step, k))
                                carry_wait(dve, b)
                                dve.copy_predicated(
                                    att[:, 4 * (b - 6):4 * (b - 5), :],
                                    level[:, 0:P].unsqueeze(1).broadcast_to([P, 4, P]),
                                    ps[:, b, :].rearrange("p (a s) -> p a s", s=P)).then_inc(psum_free[b], 1)
                        if step == "level" and 0 < k < LEVELS:
                            h, b = 2 ** (k - 1), 6 + k % 2
                            n, c0 = P // (2 * h), P + (k - 1) * P // 2
                            wait_full(dve, layer, b, (step, k))
                            wait_read(dve, layer, 7 if k == 1 else 6 + (k - 1) % 2, ("level", k - 1))
                            carry_wait(dve, 8 + k)
                            for a0 in range(0, A_HEADS * TT, 4):
                                last = dve.copy_predicated(
                                    att[:, a0:a0 + 4, :].rearrange("p a (n two h) -> p a n two h", two=2, h=h)
                                    [:, :, :, 1, :],
                                    level[:, c0:c0 + P // 2].rearrange("p (n h) -> p n h", h=h).unsqueeze(1)
                                    .broadcast_to([P, 4, n, h]),
                                    ps[:, b, a0 * P // 2:(a0 + 4) * P // 2].rearrange(
                                        "p (a n h) -> p a n h", n=n, h=h))
                            last.then_inc(psum_free[b], 1)
                        if step == "level" and k == LEVELS:
                            wait_full(dve, layer, 6, (step, k))
                            dve.tensor_copy(att01[:, :, :], ps[:, 6, :].rearrange("p (a s) -> p a s", s=P))\
                                .then_inc(psum_free[6], 1)
                        if step == "score":
                            i, bank = k % 2, 6 + k % 2
                            wait_full(dve, layer, bank, (step, k))
                            if k == 0:
                                dve.wait_ge(small_in, layer * 32 + 32)
                            dve.scalar_tensor_tensor(prob[:, i, :], ps[:, bank, 0:3 * P], SCALE,
                                                     bias[:, int(k >= B_HEADS), :], ALU.mult, ALU.add)\
                                .then_inc(psum_free[bank], 1)
                            wait_read(dve, layer, bank, (step, k))
                            for t in range(TT):
                                last = dve.reduce_max(hd[:, i, 0, t:t + 1], prob[:, i, keys[t]], AX.X)
                            link(last)
                            dve.tensor_scalar(hd[:, i, 1, :], hd[:, i, 0, :], sinks[:, k:k + 1], -1.0, ALU.max,
                                              ALU.mult).then_inc(max_done, 1)
                        if step == "finish":
                            i = k % 2
                            dve.wait_ge(exp_done, layer * N_HEADS + (k + 1))
                            link(dve.tensor_tensor(hd[:, i, 2, :], hd[:, i, 2, :], hd[:, i, 3, :], ALU.add))
                            link(dve.reciprocal(hd[:, i, 4, :], hd[:, i, 2, :]))
                            for t in range(TT):
                                last = dve.tensor_scalar(prob[:, i, keys[t]], prob[:, i, keys[t]],
                                                         hd[:, i, 4, t:t + 1], None, ALU.mult)
                            last.then_inc(prob_done, 1)
                        if step == "flip":
                            wait_full(dve, layer, 4, (step, k))
                            dve.tensor_copy(probT[:, k % 2, :], ps[:, 4, 0:3 * P]).then_inc(psum_free[4], 1)
                        if step == "hsquare":
                            wait_read(dve, layer, 7, ("hout", 0))
                            link(dve.tensor_tensor(osq, osb, osb, ALU.mult))
                            link(dve.reduce_sum(hs[:, 0, :], heads(osq), AX.X))
                            dve.tensor_scalar(hs[:, 1, :], hs[:, 0, :], 1.0 / HEAD, EPS, ALU.mult, ALU.add)\
                                .then_inc(ovar_done, 1)
                        if step == "hscale":
                            dve.wait_ge(ostd_done, layer + 1)
                            link(dve.reciprocal(hs[:, 3, :], hs[:, 2, :]))
                            link(dve.tensor_tensor(heads(osb), heads(osb), hs[:, 3, :].unsqueeze(2).broadcast_to(
                                [P, TT * A_HEADS, HEAD]), ALU.mult))
                        if step == "hgate":
                            dve.wait_ge(gate_done, layer + 1)
                            dve.tensor_tensor(osb, osb, gA[:, :, :], ALU.mult).then_inc(o_gated, 1)
                        if step == "mixsplit":
                            b = MIX_ORDER[k]
                            low_part(layer, 8 + k, 2 * b, mix[:, 2 * b:2 * b + 2, :])
                        if step == "yevac":
                            y_chunk(layer, 0, k, out_banks(k))
                last_chunk_and_norm(layer, 0)
                ffn_chunk(layer, 0, True)
                with dve.Fori(1, NC_FF) as c:
                    ffn_chunk(layer, c, False)
                for n in range(NC_OUT * GD):
                    split_lo(layer, 0, BASE_DOWN + n)
                    if n in (3, 5):
                        up(layer, NC_FF - 1, (n - 3) // 2)
                    if n in (5, 7):
                        hidden_lo(layer, NC_FF - 1, (n - 5) // 2)
                    if n >= GD and n % GD == LAG - 1:
                        y_chunk(layer, 1, n // GD - 1, in_banks(n // GD - 1))
                last_chunk_and_norm(layer, 1)
            assert link.n == DVE_LINKS, link.n
            link.base = before + DEPTH * DVE_LINKS - link.n
            dve.wait_ge(ln2_in, 32 * DEPTH)
            dve.wait_ge(ln_done, CREDIT + NORM_STEPS * 2 * DEPTH)
            dve.wait_ge(ln_act, CREDIT + 2 * DEPTH)
            for t in range(TT):
                for pieces in [FIN_DVE[t]] if t == 0 else [(piece,) for piece in FIN_DVE[t]]:
                    for c0, c1 in pieces:
                        last = dve.tensor_tensor(xres[:, t, c0:c1], xres[:, t, c0:c1], lnb[:, 0, c0:c1], ALU.mult)
                    link(last)
                    for c0, c1 in pieces:
                        dve.tensor_tensor(xres[:, t, c0:c1], xres[:, t, c0:c1], lnb[:, 1, c0:c1], ALU.add)\
                            .then_inc(fin_done, 1)

        @block.tensor
        def _(pe):
            pe.nop().then_inc(pe_used, CREDIT)
            pe.wait_ge(const_in, 16)
            pe.wait_ge(lb_in, 16)
            rows = DEPTH * A_HEADS
            pe.transpose(ps[:, 7, 0:rows], lb_rows[0:rows, :], ident[0:rows, 0:rows]).then_inc(lb_turned, 1)

            def turn_x(layer, which, order):
                for b, t in order:
                    if t == 0:
                        wait_free(pe, layer, b, ("xturn", which))
                        if which == 0 and b % 2 == 0:
                            pe.wait_ge(x_in[b // 2], 16)
                    if t == 0 and b >= 4:
                        pe.wait_ge(ln_act, layer * 2 + (which + CREDIT))
                    else:
                        step = 1 if t == 0 else (2, 3, 4, 4)[b // 2]
                        pe.wait_ge(ln_done, layer * (2 * NORM_STEPS) + (NORM_STEPS * (which - 1) + step + CREDIT))
                    for kk in range(2):
                        ins = pe.transpose(ps[:, b, kk * SEQ + t * P:kk * SEQ + (t + 1) * P],
                                           xres[:, t, (2 * b + kk) * P:(2 * b + kk + 1) * P], ident[:, :])
                    if t == TT - 1:
                        ins.then_inc(psum_full[b], 1)

            def rows_times_group(layer, n, stationary, kts, bank, t, start, stop):
                s, toks = n % RING, slice(t * P, (t + 1) * P)
                for kk, kt in enumerate(kts):
                    hi, lo = stationary[:, kt, 0, toks], stationary[:, kt, 1, toks]
                    pe.matmul(ps[:, bank, :], hi, whi[:, s, kk, :], start=start and kk == 0, stop=False)
                    pe.matmul(ps[:, bank, :], hi, wlo[:, s, kk, :], start=False, stop=False)
                    ins = pe.matmul(ps[:, bank, :], lo, whi[:, s, kk, :], start=False, stop=stop and kk == GK - 1)
                return ins

            def rows_times_chunk(layer, n, stationary, kts, banks, first, last):
                pe.wait_ge(lo_done, layer * GROUPS + (n + 1 + CREDIT))
                for t in range(TT):
                    ins = rows_times_group(layer, n, stationary, kts, banks[t], t, first, last)
                ins.then_inc(pe_used, 1)

            def skewed_end(layer, n0, stationary, pairs, banks):
                for t in range(TT):
                    for i, pair in enumerate(pairs):
                        if t == 0:
                            pe.wait_ge(lo_done, layer * GROUPS + (n0 + i + 1 + CREDIT))
                        ins = rows_times_group(layer, n0 + i, stationary, (GK * pair, GK * pair + 1), banks[t], t,
                                               False, i == SKEW - 1)
                        if t == 1:
                            ins.then_inc(pe_used, 1)
                    if t == 0:
                        ins.then_inc(first_tile, 1)

            def ffn_chunk(layer, c, first):
                for half in range(2):
                    for j in range(GC):
                        s = j % RING
                        if first and half == 0:
                            pe.wait_ge(x_ready, layer * 24 + (17 + j))
                        if j == 0 and not first:
                            pe.wait_ge((conv_done, h_full)[half], layer * PAIRS + c * 2)
                        pe.wait_ge(lo_done, layer * GROUPS + c * (2 * GC) + (BASE_FFN + half * GC + j + 1 + CREDIT))
                        for m in range(4):
                            cols = slice(m * P, (m + 1) * P)
                            bank = 4 * half + m
                            if j == 0 and first:
                                wait_read(pe, layer, bank, ("xturn", 1))
                            for kk in range(GK):
                                kt = GK * j + kk
                                for part in ((whi, wlo) if kt < KT - 1 else (wlo, whi)):
                                    if part is whi:
                                        ins = pe.matmul(ps[:, bank, :], whi[:, s, kk, cols],
                                                        xT[:, kt, :, :].rearrange("p a s -> p (a s)"),
                                                        start=kt == 0, stop=kt == KT - 1)
                                    else:
                                        ins = pe.matmul(ps[:, bank, 0:SEQ], wlo[:, s, kk, cols], xT[:, kt, 0, :],
                                                        start=False, stop=False, skip_group_check=True)
                        ins.then_inc(pe_used, 1)

            with pe.Fori(0, DEPTH) as layer:
                turn = [(2 * c + b, t) for c in range(NC_OUT) for t in range(TT) for b in range(2)]
                turn_x(layer, 0, turn[:12])
                for p in range(BASE_FFN - SKEW):
                    i, j = p // GC, p % GC
                    if p < BASE_OUT:
                        banks, kts = in_banks(i), (GK * j, GK * j + 1)
                        if i == 0:
                            pe.wait_ge(x_ready, layer * 24 + (j + 1))
                        if j == 0:
                            for b in banks:
                                wait_free(pe, layer, b, ("proj", i))
                    else:
                        c = i - NC_IN
                        banks, kts = out_banks(c), (GK * MIX_ORDER[j], GK * MIX_ORDER[j] + 1)
                        if c == 0:
                            pe.wait_ge(x_ready, layer * 24 + (9 + j))
                        if j == 0:
                            for b in banks:
                                wait_free(pe, layer, b, ("out", c))
                    rows_times_chunk(layer, p, xT, kts, banks, j == 0, j == GC - 1)
                    if p == 0:
                        turn_x(layer, 0, turn[12:])
                    for step, k in STEPS.get(p, ()):
                        if step == "params":
                            pe.wait_ge(params_in, layer * 128 + 128)
                            wait_free(pe, layer, 6, (step, k))
                            col = 0
                            for n, rows in enumerate(PAR_SETS):
                                ins = pe.transpose(ps[:, 6, col:col + rows], par_rows[0:rows, n, :],
                                                   ident[0:rows, 0:rows])
                                col += rows
                            ins.then_inc(psum_full[6], 1)
                        if step == "turn":
                            if ORDER[k] in (F_CHUNK, Q_CHUNK):
                                wait_read(pe, layer, in_banks(k)[1], ("proj", k))
                            else:
                                pe.wait_ge(rope_done, layer * (TT * len(ROPES)) + TT * (ROPES.index(k) + 1))
                            for pair in turned_pairs(ORDER[k]):
                                wait_free(pe, layer, 4 + pair, (step, k))
                                for b in range(2):
                                    for t in range(TT):
                                        c0 = (2 * pair + b) * P
                                        ins = pe.transpose(
                                            ps[:, 4 + pair, b * SEQ + t * P:b * SEQ + (t + 1) * P],
                                            staged[:, k % 2, t, c0:c0 + P], ident[:, :])
                                ins.then_inc(psum_full[4 + pair], 1)
                        if step == "level" and k == 0:
                            pe.wait_ge(f_ready, layer + 1)
                            wait_read(pe, layer, 5, ("turn", 1))
                            for b in (6, 7):
                                wait_free(pe, layer, b, (step, k))
                                for a in range(4):
                                    h, t = divmod(4 * (b - 6) + a, TT)
                                    toks = slice(t * P, (t + 1) * P)
                                    ins = pe.matmul(ps[:, b, a * P:(a + 1) * P], kT[:, h, toks], qT[:, h, toks],
                                                    start=True, stop=True)
                                ins.then_inc(psum_full[b], 1)
                        if step == "level" and 0 < k < LEVELS:
                            half, b = 2 ** (k - 1), 6 + k % 2
                            pe.wait_ge(qk_ready, layer * LEVELS + k)
                            wait_free(pe, layer, b, (step, k))
                            for a in range(A_HEADS * TT):
                                h, t = divmod(a, TT)
                                toks = slice(t * P, (t + 1) * P)
                                queries = ql[:, h, toks].rearrange("p (n two h) -> p n two h", two=2, h=half)
                                ins = pe.matmul(ps[:, b, a * P // 2:(a + 1) * P // 2], kl[:, h, toks],
                                                queries[:, :, 1, :], start=True, stop=True)
                            ins.then_inc(psum_full[b], 1)
                        if step == "level" and k == LEVELS:
                            pe.wait_ge(qk_ready, layer * LEVELS + k)
                            wait_free(pe, layer, 6, (step, k))
                            for h in range(A_HEADS):
                                ins = pe.matmul(ps[:, 6, h * P:(h + 1) * P], kl[:, h, 0:P], ql[:, h, P:SEQ],
                                                start=True, stop=True)
                            ins.then_inc(psum_full[6], 1)
                        if step == "score":
                            bank = 6 + k % 2
                            if k == 0:
                                wait_read(pe, layer, 5, ("turn", B_TURN))
                            if k == B_HEADS:
                                wait_read(pe, layer, 4, ("turn", C_TURN))
                            if k == B_HEADS + C_EARLY:
                                wait_read(pe, layer, 5, ("turn", C_TURN_LAST))
                            wait_free(pe, layer, bank, (step, k))
                            if k < B_HEADS:
                                q, key = k, B_HEADS + k
                            else:
                                q = B_HEADS + k
                                key = 2 * B_HEADS + C_HEADS + (k - B_HEADS) // (C_HEADS // C_KV)
                            for t in range(TT):
                                ins = pe.matmul(ps[:, bank, keys[t]], qkT[:, q, t * P:(t + 1) * P],
                                                qkT[:, key, 0:(t + 1) * P], start=True, stop=True)
                            ins.then_inc(psum_full[bank], 1)
                        if step == "flip":
                            pe.wait_ge(prob_done, layer * N_HEADS + (k + 1))
                            wait_free(pe, layer, 4, (step, k))
                            for n in range(3):
                                ins = pe.transpose(ps[:, 4, n * P:(n + 1) * P],
                                                   prob[:, k % 2, n * P:(n + 1) * P], ident[:, :])
                            ins.then_inc(psum_full[4], 1)
                        if step == "value":
                            if k in V_FIRST:
                                i = V_FIRST[k]
                                wait_read(pe, layer, in_banks(i)[1], ("proj", i))
                            wait_read(pe, layer, 4, ("flip", k))
                            wait_free(pe, layer, 5, (step, k))
                            v, h = (vB, k) if k < B_HEADS else (vC, (k - B_HEADS) // (C_HEADS // C_KV))
                            cols = slice(h * HEAD, (h + 1) * HEAD)
                            pT = probT[:, k % 2, :]
                            pe.matmul(ps[:, 5, 0:P], v[:, 0, cols], pT[:, 0:P], start=True, stop=True)
                            pe.matmul(ps[:, 5, P:SEQ], v[:, 0, cols], pT[:, P:2 * P], start=True, stop=False)
                            pe.matmul(ps[:, 5, P:SEQ], v[:, 1, cols], pT[:, 2 * P:3 * P], start=False, stop=True)\
                                .then_inc(psum_full[5], 1)
                        if step == "hout":
                            wait_read(pe, layer, in_banks(I_AT)[1], ("proj", I_AT))
                            wait_read(pe, layer, 7, ("level", LEVELS - 1))
                            wait_read(pe, layer, 6, ("level", LEVELS))
                            for t in range(TT):
                                wait_free(pe, layer, 6 + t, (step, k))
                                for h in range(A_HEADS):
                                    o, cols = ps[:, 6 + t, h * HEAD:(h + 1) * HEAD], slice(h * HEAD, (h + 1) * HEAD)
                                    if t == 1:
                                        pe.matmul(o, att01[:, h, :], iA[:, 0, cols], start=True, stop=False)
                                    ins = pe.matmul(o, att[:, h * TT + t, :], iA[:, t, cols], start=t == 0,
                                                    stop=True)
                                ins.then_inc(psum_full[6 + t], 1)
                        if step == "hturn":
                            pe.wait_ge(o_gated, layer + 1)
                            for pair in range(2):
                                wait_free(pe, layer, 4 + pair, (step, k))
                                for b in range(2):
                                    for t in range(TT):
                                        c0 = (2 * pair + b) * P
                                        ins = pe.transpose(
                                            ps[:, 4 + pair, b * SEQ + t * P:b * SEQ + (t + 1) * P],
                                            osb[:, t, c0:c0 + P], ident[:, :])
                                ins.then_inc(psum_full[4 + pair], 1)
                skewed_end(layer, BASE_FFN - SKEW, xT, MIX_ORDER[-SKEW:], out_banks(NC_OUT - 1))
                late = out_banks(NC_OUT - 1)[1]
                turn_x(layer, 1, [(b, 0) for b in range(8) if b != late] + [(late, 0)] + [(b, 1) for b in range(8)])
                ffn_chunk(layer, 0, True)
                with pe.Fori(1, NC_FF) as c:
                    ffn_chunk(layer, c, False)
                for n in range(NC_OUT * GD - SKEW):
                    c, j = n // GD, n % GD
                    if n == 0:
                        pe.wait_ge(conv_done, layer * PAIRS + PAIRS)
                        pe.wait_ge(h_done, layer * PAIRS + (PAIRS - 2))
                    if n in (GD - 2, GD - 1):
                        pe.wait_ge(h_done, layer * PAIRS + (PAIRS - GD + n + 1))
                    if j == 0:
                        for b in in_banks(c):
                            wait_free(pe, layer, b, ("down", c))
                    rows_times_chunk(layer, BASE_DOWN + n, hT, (GK * j, GK * j + 1), in_banks(c), j == 0,
                                     j == GD - 1)
                skewed_end(layer, GROUPS - SKEW, hT, range(GD - SKEW, GD), in_banks(NC_OUT - 1))


def attention_bias():
    lag = np.arange(SEQ)[:, None] - np.arange(SEQ)[None, :]
    count = sum(((lag >= 0) & (lag % d == 0) & (lag // d <= w // d)).astype(np.float64) for w, d in PATTERNS)
    window = (lag >= 0) & (lag < C_WINDOW)
    log_count = np.where(count > 0, np.log(np.maximum(count, 1)), NEG)
    both = np.stack([log_count, np.where(window, 0.0, NEG)]).astype(np.float32)
    return np.concatenate([both[:, 0:P, 0:P], both[:, P:SEQ, :]], axis=2)


def level_masks():
    j, i = np.arange(P)[:, None], np.arange(P)[None, :]
    masks = [j == i]
    for n in range(1, LEVELS):
        h = 2 ** (n - 1)
        second = [q for q in range(P) if q // h % 2 == 1]
        masks.append(((j // (2 * h) == i // (2 * h)) & (j // h % 2 == 0))[:, second])
    return np.concatenate(masks, axis=1).astype(np.float32)


def rope_tables():
    inv = np.float32(ROPE_THETA) ** (-np.arange(0, ROPE, 2, dtype=np.float32) / np.float32(ROPE))
    angle = (np.arange(SEQ, dtype=np.float32)[:, None] * inv.astype(np.float32)[None, :]).astype(np.float64)
    cos, sin = np.cos(angle), np.sin(angle)
    return np.stack([np.concatenate([cos, cos], 1), np.concatenate([-sin, sin], 1)]).astype(np.float32)


_INS = ["x", "w_in", "lb_logits", "a_norm_w", "c_sinks", "w_out", "ln1_g", "ln1_b", "w_gate", "w_up", "conv_w",
        "conv_b", "w_down", "ln2_g", "ln2_b"]


def kernel(**inputs):
    import numpy as _np
    import concourse.bacc as _bacc
    from concourse import mybir as _mybir
    from concourse.bass_utils import run_bass_kernel_spmd as _run

    nc = _bacc.Bacc("TRN2", target_bir_lowering=False, num_devices=1)
    arrays, args = {}, []
    values = [(name, _np.ascontiguousarray(inputs[name])) for name in _INS]
    values += [("c_ident", _np.eye(P, dtype=_np.float32)), ("c_bias", attention_bias()),
               ("c_level", level_masks()), ("c_rope", rope_tables())]
    for name, a in values:
        arrays[f"in_{name}_dram"] = a
        args.append(nc.dram_tensor(f"in_{name}_dram", a.shape, _mybir.dt.from_np(a.dtype), kind="ExternalInput").ap())
    args.append(nc.dram_tensor("out_0_dram", (1, SEQ, D_MODEL), _mybir.dt.float32, kind="ExternalOutput").ap())
    program(nc, *args)
    r = _run(nc, [arrays], core_ids=[0])
    return r.results[0]["out_0_dram"]
```
